# Optimizing a Trainium2 kernel written in Bass

```python
import math
import jax, jax.numpy as jnp
from jax import lax
import numpy as np

D_MODEL = 1024
BATCH = 1
SEQ = 512
DEPTH = 1

N_HEADS = 8
HEAD_DIM = 64
ATTN_WIDTH = N_HEADS * HEAD_DIM
KV_DIM = HEAD_DIM
N_IDX_HEADS = 8
IDX_DIM = 32
TOPK_KEYS_MAX = 256
Q_BLOCK = 128
POOL_WINDOWS = (2, 4, 8, 16)
N_POOL_GROUPS = 4
POOL_GROUP_DIM = 128
POOL_WIDTH = N_POOL_GROUPS * POOL_GROUP_DIM
N_BRANCHES = 2
IN_COLS = ATTN_WIDTH + 2 * KV_DIM + N_IDX_HEADS * IDX_DIM + IDX_DIM + N_IDX_HEADS + POOL_WIDTH + N_BRANCHES * D_MODEL
N_EXPERTS = 32
EXPERT_TOP_K = 4
D_EXPERT = D_MODEL
SWIGLU_ALPHA = 1.702
SWIGLU_LIMIT = 7.0
EXPERT_BLOCK = 128
RMS_EPS = 1e-5
NEG_INF = -1e30

kernel_name = "hybrid_dsa_pool_moe_block"

def rmsnorm(x, g):
    xf = x.astype(jnp.float32)
    y = xf * lax.rsqrt(jnp.mean(xf * xf, axis=-1, keepdims=True) + RMS_EPS)
    return (y * g.astype(jnp.float32)).astype(x.dtype)

def split_columns(proj):
    sizes = (ATTN_WIDTH, KV_DIM, KV_DIM, N_IDX_HEADS * IDX_DIM, IDX_DIM, N_IDX_HEADS,
             POOL_WIDTH, D_MODEL, D_MODEL)
    offs = [int(o) for o in np.cumsum(sizes)[:-1]]
    return jnp.split(proj, offs, axis=-1)

def dsa_attention(q, k, v, iq, ik, iw):
    B, S = q.shape[0], q.shape[1]
    n_keys = min(TOPK_KEYS_MAX, S // 4)
    nqb = S // Q_BLOCK
    f32 = jnp.float32
    key_pos = jnp.arange(S)
    ikf = ik.astype(f32)
    gather_rows = jax.vmap(lambda a, i: a[i])

    def to_blocks(a):
        return jnp.moveaxis(a.reshape((B, nqb, Q_BLOCK) + a.shape[2:]), 1, 0)

    def one_block(args):
        qb, iqb, iwb, q0 = args
        qpos = q0 + jnp.arange(Q_BLOCK)
        causal = key_pos[None, :] <= qpos[:, None]
        rel = jax.nn.relu(jnp.einsum('bqhd,bsd->bqhs', iqb.astype(f32), ikf))
        score = jnp.einsum('bqh,bqhs->bqs', iwb.astype(f32), rel)
        score = jnp.where(causal[None], score, NEG_INF)
        _, sel = lax.top_k(score, n_keys)
        ks = gather_rows(k, sel).astype(f32)
        vs = gather_rows(v, sel).astype(f32)
        valid = sel <= qpos[None, :, None]
        logits = jnp.einsum('bqhd,bqkd->bqhk', qb.astype(f32), ks) * (HEAD_DIM ** -0.5)
        logits = jnp.where(valid[:, :, None, :], logits, NEG_INF)
        p = jax.nn.softmax(logits, axis=-1)
        return jnp.einsum('bqhk,bqkd->bqhd', p, vs).astype(q.dtype)

    out = lax.map(one_block, (to_blocks(q), to_blocks(iq), to_blocks(iw),
                              jnp.arange(nqb) * Q_BLOCK))
    return jnp.moveaxis(out, 0, 1).reshape(B, S, ATTN_WIDTH)

def multiscale_pool(u, w_pool, pool_scale):
    B, S, _ = u.shape
    uf = u.astype(jnp.float32)
    csum = jnp.cumsum(uf, axis=1)
    t = jnp.arange(S)
    means = []
    for gi, win in enumerate(POOL_WINDOWS):
        cg = csum[..., gi * POOL_GROUP_DIM:(gi + 1) * POOL_GROUP_DIM]
        shifted = jnp.pad(cg, ((0, 0), (win, 0), (0, 0)))[:, :S]
        count = jnp.minimum(t + 1, win).astype(jnp.float32)[None, :, None]
        means.append((cg - shifted) / count)
    pooled = jnp.stack(means, axis=2) - uf.reshape(B, S, N_POOL_GROUPS, POOL_GROUP_DIM)
    mixed = jnp.einsum('bsgc,gcd->bsgd', pooled, w_pool.astype(jnp.float32)).reshape(B, S, POOL_WIDTH)
    return (mixed * pool_scale.astype(jnp.float32)).astype(u.dtype)

def expert_ffn(h, w_router, b_router, w_gate_up, b_gate_up, w_down, b_down):
    B, S, D = h.shape
    T = B * S
    f32 = jnp.float32
    xt = h.reshape(T, D)
    logits = xt.astype(f32) @ w_router.astype(f32) + b_router.astype(f32)
    top_val, top_idx = lax.top_k(logits, EXPERT_TOP_K)
    gate = jax.nn.softmax(top_val, axis=-1)
    A = T * EXPERT_TOP_K
    flat_e = top_idx.reshape(A)
    flat_tok = jnp.arange(A, dtype=jnp.int32) // EXPERT_TOP_K
    flat_g = gate.reshape(A)
    order = jnp.argsort(flat_e)
    se = flat_e[order]
    counts = jnp.bincount(flat_e, length=N_EXPERTS)
    blocks_per = (counts + EXPERT_BLOCK - 1) // EXPERT_BLOCK
    block_end = jnp.cumsum(blocks_per)
    block_start = block_end - blocks_per
    row_start = jnp.cumsum(counts) - counts
    rank = jnp.arange(A) - row_start[se]
    dest = block_start[se] * EXPERT_BLOCK + rank
    nb = A // EXPERT_BLOCK + N_EXPERTS
    P = nb * EXPERT_BLOCK
    row_tok = jnp.full((P,), T, jnp.int32).at[dest].set(flat_tok[order])
    row_g = jnp.zeros((P,), f32).at[dest].set(flat_g[order])
    blk_e = jnp.minimum(jnp.searchsorted(block_end, jnp.arange(nb), side='right'), N_EXPERTS - 1)
    xs = jnp.take(xt, row_tok, axis=0, mode='fill', fill_value=0).reshape(nb, EXPERT_BLOCK, D)

    def expert_block(args):
        xb, e = args
        gu = xb.astype(f32) @ w_gate_up[e].astype(f32) + b_gate_up[e].astype(f32)
        g, u = gu[:, 0::2], gu[:, 1::2]
        g = jnp.minimum(g, SWIGLU_LIMIT)
        u = jnp.clip(u, -SWIGLU_LIMIT, SWIGLU_LIMIT)
        act = (u + 1.0) * (g * jax.nn.sigmoid(SWIGLU_ALPHA * g))
        return act @ w_down[e].astype(f32) + b_down[e].astype(f32)

    ys = lax.map(expert_block, (xs, blk_e)).reshape(P, D)
    out = jax.ops.segment_sum(ys * row_g[:, None], row_tok, num_segments=T)
    return out.reshape(B, S, D).astype(h.dtype)

def setup_inputs(seed: int = 0) -> dict:
    key = jax.random.key(seed)
    ks = jax.random.split(key, 17)
    n = jax.random.normal
    f = jnp.float32
    F2 = 2 * D_EXPERT
    return {
        "x": n(ks[0], (BATCH, SEQ, D_MODEL), f),
        "norm_mix": 1.0 + 0.1 * n(ks[1], (DEPTH, D_MODEL), f),
        "w_in": n(ks[2], (DEPTH, D_MODEL, IN_COLS), f) * D_MODEL ** -0.5,
        "w_pool": n(ks[3], (DEPTH, N_POOL_GROUPS, POOL_GROUP_DIM, POOL_GROUP_DIM), f) * POOL_GROUP_DIM ** -0.5,
        "pool_scale": 1.0 + 0.1 * n(ks[4], (DEPTH, POOL_WIDTH), f),
        "w_attn_up": n(ks[5], (DEPTH, ATTN_WIDTH, D_MODEL), f) * ATTN_WIDTH ** -0.5,
        "w_pool_up": n(ks[6], (DEPTH, POOL_WIDTH, D_MODEL), f) * POOL_WIDTH ** -0.5,
        "w_out": n(ks[7], (DEPTH, D_MODEL, D_MODEL), f) * D_MODEL ** -0.5,
        "norm_ffn": 1.0 + 0.1 * n(ks[8], (DEPTH, D_MODEL), f),
        "w_router": n(ks[9], (DEPTH, D_MODEL, N_EXPERTS), f) * D_MODEL ** -0.5,
        "b_router": 0.01 * n(ks[10], (DEPTH, N_EXPERTS), f),
        "w_gate_up": n(ks[11], (DEPTH, N_EXPERTS, D_MODEL, F2), f) * D_MODEL ** -0.5,
        "b_gate_up": 0.02 * n(ks[12], (DEPTH, N_EXPERTS, F2), f),
        "w_down": n(ks[13], (DEPTH, N_EXPERTS, D_EXPERT, D_MODEL), f) * D_EXPERT ** -0.5,
        "b_down": 0.02 * n(ks[14], (DEPTH, N_EXPERTS, D_MODEL), f),
        "norm_final": 1.0 + 0.1 * n(ks[15], (D_MODEL,), f),
    }

def reference(x, norm_mix, w_in, w_pool, pool_scale, w_attn_up, w_pool_up, w_out, norm_ffn,
              w_router, b_router, w_gate_up, b_gate_up, w_down, b_down, norm_final):
    B, S, _ = x.shape
    idx_w_scale = (N_IDX_HEADS ** -0.5) * (IDX_DIM ** -0.5)
    for l in range(DEPTH):
        h = rmsnorm(x, norm_mix[l])
        proj = h @ w_in[l]
        q, k, v, iq, ik, iw, u, ga, gp = split_columns(proj)
        q = q.reshape(B, S, N_HEADS, HEAD_DIM)
        iq = iq.reshape(B, S, N_IDX_HEADS, IDX_DIM)
        iw = iw * idx_w_scale
        y_attn = dsa_attention(q, k, v, iq, ik, iw)
        y_pool = multiscale_pool(u, w_pool[l], pool_scale[l])
        mixed = (jax.nn.sigmoid(ga) * (y_attn @ w_attn_up[l])
                 + jax.nn.sigmoid(gp) * (y_pool @ w_pool_up[l]))
        x = x + mixed @ w_out[l]
        h2 = rmsnorm(x, norm_ffn[l])
        x = x + expert_ffn(h2, w_router[l], b_router[l], w_gate_up[l], b_gate_up[l], w_down[l], b_down[l])
    return rmsnorm(x, norm_final)


_drawn_inputs = setup_inputs


def setup_inputs(seed=0):
    import zlib

    import numpy as np

    out = dict(_drawn_inputs(seed))
    spreads = {}
    factors = {'b_gate_up': 5.502, 'b_down': 6.401}
    for name, (base, spread) in spreads.items():
        noise = np.random.default_rng([zlib.crc32(name.encode()), seed]).standard_normal(out[name].shape)
        drawn = base * np.exp(spread * noise) if base else spread * noise
        out[name] = __import__('jax').numpy.asarray(drawn.astype(out[name].dtype))
    for name, factor in factors.items():
        out[name] = (out[name] * factor).astype(out[name].dtype)
    return out
```

```python
from contextlib import ExitStack

import concourse.bass as bass
from concourse import mybir

ALU = mybir.AluOpType
ACT = mybir.ActivationFunctionType
AX_X = mybir.AxisListType.X
F32 = mybir.dt.float32
BF16 = mybir.dt.bfloat16
F32R = mybir.dt.float32r
I32 = mybir.dt.int32
U32 = mybir.dt.uint32

P = 128
CAP = 96
NH, DH = 8, 64
NI, DI = 8, 32
TOPK_KEYS_MAX = 256
WINDOWS = (2, 4, 8, 16)
TOPE = 4
ALPHA, LIMIT = 1.702, 7.0
EPS = 1e-5
NEG = -1e30
TAKEN = -3e38
PAD = WINDOWS[-1]
RING = 12
SPLIT = 3


def hybrid_block(nc, x, norm_mix, w_in, w_pool, pool_scale, w_attn_up, w_pool_up, w_out, norm_ffn,
                 w_router, b_router, w_gate_up, b_gate_up, w_down, b_down, norm_final,
                 h2_dram, table_dram, y_dram, out):
    _, T, D = x.shape
    E = w_router.shape[2]
    F2 = w_gate_up.shape[3]
    F = F2 // 2
    NT = T // P
    KC = D // P
    AW = NH * DH
    NG = len(WINDOWS)
    NKEYS = min(TOPK_KEYS_MAX, T // 4)
    NROUND = NKEYS // 8
    BLOCKS = -(-T // CAP)
    SLOTS = BLOCKS * CAP
    EXTRA = T * TOPE // CAP
    CAND = E * (BLOCKS - 1)
    KVCOL = AW
    IQCOL = KVCOL + 2 * DH
    IKCOL = IQCOL + NI * DI
    UCOL = IKCOL + DI + NI
    GCOL = UCOL + NG * P
    Q_PIECES, U_PIECE, G_PIECE = AW // P, 8, 12
    N_PROJ = G_PIECE + 2 * KC
    N_UP = KC
    N_OUT = 2 * (KC // 2)
    N_PIECES = N_PROJ + N_UP + N_OUT
    STEP = 12
    assert KC == 8 and NT == 4 and F == D and NKEYS == P and DH == 64 and NG == NT and 2 * E == 64

    x_t = x[0].rearrange("(t p) d -> t p d", p=P)
    out_t = out[0].rearrange("(t p) d -> t p d", p=P)
    w_in_c = w_in[0].rearrange("(c p) n -> p c n", p=P)
    w_au_c = w_attn_up[0].rearrange("(c p) n -> p c n", p=P)
    w_pu_c = w_pool_up[0].rearrange("(c p) n -> p c n", p=P)
    w_out_c = w_out[0].rearrange("(c p) n -> p c n", p=P)
    w_gu_c = w_gate_up[0].rearrange("e (c p) n -> p e c n", p=P)
    w_dn_c = w_down[0].rearrange("e (c p) n -> p e c n", p=P)
    h2_t = h2_dram.rearrange("(t p) d -> t p d", p=P)
    y_t = y_dram[0:T * TOPE, :].rearrange("(t p k) d -> t p (k d)", p=P, k=TOPE)
    table_init = table_dram.rearrange("(b s e) w -> s b (e w)", b=BLOCKS, e=E)
    table_blk = table_dram.rearrange("(b s e) w -> s b e w", b=BLOCKS, e=E)
    DOWN = STEP - 4

    with ExitStack() as ctx:
        def sem(name):
            return ctx.enter_context(nc.semaphore(name))

        def place(stack, name, shape, dt=F32):
            return stack.enter_context(nc.sbuf_tensor(name, shape, dt))

        ps = ctx.enter_context(nc.psum_tensor("ps", [P, 8, 512], F32))

        ident = place(ctx, "ident", [P, P])
        expert_id = place(ctx, "expert_id", [2 * E, E])
        sel_up = place(ctx, "sel_up", [2 * E, CAP], F32R)
        sel_down = place(ctx, "sel_down", [2 * E, CAP], F32R)
        gather_tab = place(ctx, "gather_tab", [CAP, 4], U32)
        y_tab = place(ctx, "y_tab", [CAP, 4], U32)
        extra_list = place(ctx, "extra_list", [1, 3, 32], I32)
        sums = place(ctx, "sums", [P, 3, NT])
        half_sums = place(ctx, "half_sums", [P, NT])
        rstd = place(ctx, "rstd", [P, 3, NT])
        half = place(ctx, "half", [P, 1])
        payload = place(ctx, "payload", [P, NT * TOPE, 4], U32)
        dest = place(ctx, "dest", [P, NT * TOPE], U32)
        start_tab = place(ctx, "start_tab", [CAP, 2], U32)

        with ExitStack() as a1:
            xTh = place(a1, "xTh", [P, KC, T], F32R)
            xTl = place(a1, "xTl", [P, KC, T], F32R)
            gates = place(a1, "gates", [P, 2 * KC, T])
            wraw = place(a1, "wraw", [P, 2, 4096])
            prob = place(a1, "prob", [P, 2, 4, T])
            with ExitStack() as a0:
                whi = place(a0, "whi", [P, 4, 1024], F32R)
                wlo = place(a0, "wlo", [P, 4, 1024], F32R)
            h2N = place(a1, "h2N", [P, NT, D])
            h2T_right = place(a1, "h2T_right", [P, KC // 2, T])
            place(a1, "rest_of_wlo", [P, 2, 1024])
            with ExitStack() as par:
                g_ffn = place(par, "g_ffn", [P, D])
                wr = place(par, "wr", [P, KC, E])
                wp = place(par, "wp", [P, NG, P])
                br = place(par, "br", [P, E])
                g_mix = place(par, "g_mix", [P, KC])
                g_ffc = place(par, "g_ffc", [P, KC])
                p_scale = place(par, "p_scale", [P, NG])
                diag = place(par, "diag", [P, P])
                tri = place(par, "tri", [P, P], BF16)
                ones = place(par, "ones", [P, P], BF16)
                e_row = place(par, "e_row", [P, E])
                with ExitStack() as a2:
                    qT = place(a2, "qT", [P, Q_PIECES, T])
                    kT = place(a2, "kT", [P, T])
                    vT = place(a2, "vT", [P, T])
                    iqT = place(a2, "iqT", [P, 2, T])
                    ikT = place(a2, "ikT", [P, T])
                    uT = place(a2, "uT", [P, NG, PAD + T])
                    win = place(a2, "win", [P, 2, PAD + T])
                    inv_n = place(a2, "inv_n", [P, NG, PAD])
                    v_sb = place(a2, "v_sb", [P, NT, DH])
                    iw = place(a2, "iw", [P, NT, NI])
                    score = place(a2, "score", [P, NT - 1, T])
                    top8 = place(a2, "top8", [P, 8])
                    pT = place(a2, "pT", [P, 2, T])
                    yN = place(a2, "yN", [P, AW])
                    nmax = place(a2, "nmax", [P, 2, 4])
                    psumx = place(a2, "psumx", [P, 2, NH])
                    pinv = place(a2, "pinv", [P, NH])
                with ExitStack() as a3:
                    mTh = place(a3, "mTh", [P, KC, T], F32R)
                    mTl = place(a3, "mTl", [P, KC, T], F32R)
                    t_at = place(a3, "t_at", [P, T])
                    t_po = place(a3, "t_po", [P, T])
                    h2T_left = place(a3, "h2T_left", [P, KC // 2, T])
                with ExitStack() as a4:
                    limit = place(a4, "limit", [P, CAND])
                    code = place(a4, "code", [P, 2, CAND])
                    over = place(a4, "over", [P, CAND])
                    rank = place(a4, "rank", [P, CAND])
                    picked = place(a4, "picked", [P, CAND])
                    pick2 = place(a4, "pick2", [P, 2, CAND])
                    rank_id = place(a4, "rank_id", [P, 1])
                    found = place(a4, "found", [P, 3])
                    cnt = place(a4, "cnt", [P, E])
                    prod = place(a4, "prod", [P, NT * TOPE, E])
                    dest_f = place(a4, "dest_f", [P, NT * TOPE])
                    lg = place(a4, "lg", [P, NT, E])
                    v8 = place(a4, "v8", [P, NT, 8])
                    i8 = place(a4, "i8", [P, NT, 8], U32)
                    i4 = place(a4, "i4", [P, NT * TOPE])
                    hot = place(a4, "hot", [P, NT * TOPE, E])
                    mask = place(a4, "mask", [P, NT, E], BF16)
                    dpos = place(a4, "dpos", [P, NT, E])
                    nv0 = place(a4, "nv0", [P, NT])
                    ex = place(a4, "ex", [P, NT, TOPE])
                    exs = place(a4, "exs", [P, NT])
                    exr = place(a4, "exr", [P, NT])
                    token_id = place(a4, "token_id", [P, NT])
                    place_id = place(a4, "place_id", [P, CAP])
                    start_tok = place(a4, "start_tok", [P, 2, NT])
                    start_sel = place(a4, "start_sel", [P, 2, NT, CAP])
        hN = gates[:, 0:KC, :].rearrange("p a b -> p (a b)").rearrange("p (t d) -> p t d", t=NT)
        xN = gates[:, KC:2 * KC, :].rearrange("p a b -> p (a b)").rearrange("p (t d) -> p t d", t=NT)
        table0 = prob[0:CAP, 1, :, :].rearrange("p a b -> p (a b)")[:, 0:BLOCKS * E * 4].bitcast(U32).rearrange("s (b e w) -> s b e w", b=BLOCKS, e=E)

        with ExitStack() as f1:
            raw = place(f1, "raw", [P, RING, 2048])
            X = place(f1, "X", [P, NT, D])
            hi = place(f1, "hi", [P, SPLIT, 2048], F32R)
            lo = place(f1, "lo", [P, SPLIT, 2048], F32R)
            xy = place(f1, "xy", [CAP, D])
            xeh = place(f1, "xeh", [P, KC, CAP], F32R)
            xel = place(f1, "xel", [P, KC, CAP], F32R)
            gu = place(f1, "gu", [CAP, 3, F])
            aTh = place(f1, "aTh", [P, KC, CAP], F32R)
            aTl = place(f1, "aTl", [P, KC, CAP], F32R)
            bias = place(f1, "bias", [2 * E, F2 + D], F32R)
        bias_raw = gu[0:2 * E, :, :].rearrange("p a b -> p (a b)")
        g_lin, g_act, u_lin = gu[:, 0, :], gu[:, 1, :], gu[:, 2, :]
        ytile = [raw[:, 2 * t:2 * t + 2, :].rearrange("p a b -> p (a b)") for t in range(NT)]
        g_fin = raw[:, 8, 0:D]

        x_in = [sem(f"x_in{t}") for t in range(NT)]
        small_in = sem("small_in")
        wgroup_in = [sem("wgroup_in0"), sem("wgroup_in1")]
        const_ready = sem("const_ready")
        inv_ready = sem("inv_ready")
        tri_step = sem("tri_step")
        diag_step = sem("diag_step")
        id_step = sem("id_step")
        tab_set = sem("tab_set")
        table_inited = sem("table_inited")
        squares = sem("squares")
        mean_ready = sem("mean_ready")
        rstd_ready = sem("rstd_ready")
        h_ready = sem("h_ready")
        h_turned = sem("h_turned")
        xT_hi = sem("xT_hi")
        xT_lo = sem("xT_lo")
        hi_done = sem("hi_done")
        lo_done = sem("lo_done")
        piece_done = sem("piece_done")
        evac_dve = sem("evac_dve")
        evac_act = sem("evac_act")
        v_turned = sem("v_turned")
        v_ready = sem("v_ready")
        idx_done = sem("idx_done")
        relu_done = sem("relu_done")
        score_step = sem("score_step")
        topk_step = sem("topk_step")
        win_step = sem("win_step")
        pooled = sem("pooled")
        pool_mixed = sem("pool_mixed")
        pool_hi = sem("pool_hi")
        pool_lo = sem("pool_lo")
        logits_done = sem("logits_done")
        masked = sem("masked")
        max_found = sem("max_found")
        nmax_ready = sem("nmax_ready")
        exp_done = sem("exp_done")
        p_turned = sem("p_turned")
        pT_even = sem("pT_even")
        pT_odd = sem("pT_odd")
        pv_done = sem("pv_done")
        pinv_ready = sem("pinv_ready")
        y_norm = sem("y_norm")
        y_turned = sem("y_turned")
        y_hi = sem("y_hi")
        y_lo = sem("y_lo")
        gated_a = sem("gated_a")
        gated_p = sem("gated_p")
        mix_sum = sem("mix_sum")
        mT_hi = sem("mT_hi")
        mT_lo = sem("mT_lo")
        x_again = sem("x_again")
        out_mm = sem("out_mm")
        x2_left = sem("x2_left")
        x2_right = sem("x2_right")
        half_squares = sem("half_squares")
        half_mean = sem("half_mean")
        wr_scaled = sem("wr_scaled")
        logits_out = sem("logits_out")
        logits_turned = sem("logits_turned")
        h2_ready = sem("h2_ready")
        h2_stored = sem("h2_stored")
        h2_turned = sem("h2_turned")
        router_mm = sem("router_mm")
        route = sem("route")
        exp_gate = sem("exp_gate")
        mask_ready = sem("mask_ready")
        pos_mm = sem("pos_mm")
        payload_ready = sem("payload_ready")
        payload_set = sem("payload_set")
        start_step = sem("start_step")
        start_mm = sem("start_mm")
        start_ready = sem("start_ready")
        table_done = sem("table_done")
        extra_step = sem("extra_step")
        extra_mm = sem("extra_mm")
        extra_ready = sem("extra_ready")
        bias_in = sem("bias_in")
        bias_hi = sem("bias_hi")
        bias_lo = sem("bias_lo")
        raw_in = [sem(f"raw_in{s}") for s in range(RING)]
        ehi_done = sem("ehi_done")
        elo_done = sem("elo_done")
        chunk_used = sem("chunk_used")
        up_bias_used = sem("up_bias_used")
        down_bias_used = sem("down_bias_used")
        sel_up_ready = sem("sel_up_ready")
        sel_down_ready = sem("sel_down_ready")
        y_all = sem("y_all")
        pool_held = sem("pool_held")
        pair_sum = sem("pair_sum")
        pu_in = [sem("pu_in0"), sem("pu_in1")]
        h2T_act = sem("h2T_act")
        h2T_dve = sem("h2T_dve")
        extra_fill = sem("extra_fill")
        inv_step = sem("inv_step")
        mask_out = sem("mask_out")
        diag_added = sem("diag_added")
        gtab_in = sem("gtab_in")
        ytab_in = sem("ytab_in")
        rows_in = sem("rows_in")
        rows_turned = sem("rows_turned")
        xe_hi = sem("xe_hi")
        xe_lo = sem("xe_lo")
        gu_done = sem("gu_done")
        g_clip = sem("g_clip")
        u_clip = sem("u_clip")
        g_sig = sem("g_sig")
        u_one = sem("u_one")
        g_gated = sem("g_gated")
        act_ready = sem("act_ready")
        act_turned = sem("act_turned")
        aT_hi = sem("aT_hi")
        aT_lo = sem("aT_lo")
        down_done = sem("down_done")
        y_scaled = sem("y_scaled")
        y_out = sem("y_out")
        yt_in = [sem(f"yt_in{t}") for t in range(NT)]
        gfin_in = sem("gfin_in")
        comb = sem("comb")
        o_ready = sem("o_ready")
        out_stored = sem("out_stored")

        block = ctx.enter_context(nc.Block())

        def raw_piece(i):
            group = wraw[:, (i // 4) % 2, :].rearrange("p (c n) -> p c n", c=KC)
            j = i % 4
            if i < N_PROJ + N_UP:
                return group[:, :, j * P:(j + 1) * P]
            return group[:, 2 * j:2 * j + 2, :]

        def split_piece(w, i):
            n = KC if i < N_PROJ + N_UP else 2
            return w[:, i % 4, :].rearrange("p (c n) -> p c n", c=n)

        def slot_of(off):
            return off % RING

        def half_of(off):
            return off % SPLIT

        def at_least(eng, which, value):
            if not (isinstance(value, int) and value <= 0):
                eng.wait_ge(which, value)

        attn = [(t, g) for t in range(NT) for g in range(2)]
        blocks_to = [0]
        for t, _ in attn:
            blocks_to.append(blocks_to[-1] + t + 1)
        N_PT = blocks_to[-1]

        def pT_evacuated(eng, n):
            eng.wait_ge(pT_odd if n % 2 else pT_even, n // 2 + 1)

        def selected(t):
            m = diag[:] if t == 0 else score[:, t - 1, 0:P * (t + 1)]
            return m.unsqueeze(1).to_broadcast([P, 4, P * (t + 1)])

        def turn_bank(c):
            return 4 + c if c < KC // 2 else (c + 1) % 8

        def h2T(c):
            return h2T_left[:, c, :] if c < KC // 2 else h2T_right[:, c - KC // 2, :]

        @block.sync
        def _(sp):
            for t in range(NT):
                sp.dma_start(xN[:, t, :], x_t[t]).then_inc(x_in[t], 16)

            def group(g):
                if g >= 2:
                    sp.wait_ge(lo_done, 4 * (g - 1))
                dst = wraw[:, g % 2, :].rearrange("p (c n) -> p c n", c=KC)
                done = wgroup_in[g % 2]
                if g < 2:
                    sp.dma_start(dst, w_in_c[:, :, 512 * g:512 * g + 512]).then_inc(done, 16)
                elif g < 7:
                    c0 = UCOL + 512 * (g - 2)
                    sp.dma_start(dst, w_in_c[:, :, c0:c0 + 512]).then_inc(done, 16)
                elif g < 9:
                    c0 = 512 * (g - 7)
                    sp.dma_start(dst[:, 0:4, :], w_au_c[:, :, c0:c0 + 512]).then_inc(done, 16)
                    sp.dma_start(dst[:, 4:8, :], w_pu_c[:, :, c0:c0 + 512]).then_inc(pu_in[g - 7], 16)
                else:
                    c0 = 512 * (g - 9)
                    sp.dma_start(dst, w_out_c[:, :, c0:c0 + 512]).then_inc(done, 16)

            group(0)
            sp.dma_start(g_mix[:], norm_mix[0].rearrange("(c p) -> p c", p=P),
                         allow_slow_non_contiguous=True).then_inc(small_in, 16)
            sp.dma_start(g_ffc[:], norm_ffn[0].rearrange("(c p) -> p c", p=P),
                         allow_slow_non_contiguous=True).then_inc(small_in, 16)
            sp.dma_start(p_scale[:], pool_scale[0].rearrange("(c p) -> p c", p=P),
                         allow_slow_non_contiguous=True).then_inc(small_in, 16)
            sp.dma_start(wp[:], w_pool[0].rearrange("g c d -> c g d")).then_inc(small_in, 16)
            sp.dma_start(wr[:], w_router[0].rearrange("(c p) e -> p c e", p=P)).then_inc(small_in, 16)
            sp.dma_start(br[:], b_router[0].partition_broadcast(P)).then_inc(small_in, 16)
            sp.dma_start(g_ffn[:], norm_ffn[0].partition_broadcast(P)).then_inc(small_in, 16)
            for g in range(1, 9):
                group(g)
            sp.wait_ge(p_turned, N_PT)
            for t in range(NT):
                sp.dma_start(X[:, t, :], x_t[t]).then_inc(x_again, 16)
            for g in range(9, 11):
                group(g)

            def load_up(e, k, u, off):
                at_least(sp, elo_done, u * STEP + (off - RING + 1))
                sp.dma_start(raw[:, slot_of(off), :].unsqueeze(1), w_gu_c[:, bass.ds(e, 1), k, :])\
                  .then_inc(raw_in[slot_of(off)], 16)

            def load_down(e, k, u, off):
                at_least(sp, elo_done, u * STEP + (off - RING + 1))
                sp.dma_start(raw[:, slot_of(off), :].rearrange("p (a c n) -> p a c n", a=1, c=2),
                             w_dn_c[:, bass.ds(e, 1), 2 * k:2 * k + 2, :]).then_inc(raw_in[slot_of(off)], 16)

            sp.wait_ge(piece_done, N_PROJ + N_UP)
            sp.wait_ge(mix_sum, N_UP)
            for k in range(DOWN):
                load_up(0, k, 0, k)
            sp.wait_ge(lo_done, N_PIECES)
            for k in range(4):
                load_up(1, k, 1, k - 4)
            for t in range(NT):
                sp.wait_ge(h2_ready, t + 1)
                sp.dma_start(h2_t[t], h2N[:, t, :]).then_inc(h2_stored, 16)
            for half_rows in range(2):
                r = slice(E * half_rows, E * half_rows + E)
                sp.dma_start(bias_raw[r, 0:F2], b_gate_up[0]).then_inc(bias_in, 16)
                sp.dma_start(bias_raw[r, F2:F2 + D], b_down[0]).then_inc(bias_in, 16)
            for k in range(4, DOWN):
                load_up(1, k, 1, k - 4)
            for k in range(4):
                load_down(0, k, 1, k + 4)
            with sp.Fori(2, E) as u:
                for k in range(DOWN):
                    load_up(u, k, u, k - 4)
                for k in range(4):
                    load_down(u - 1, k, u, k + 4)
            for k in range(4):
                load_down(E - 1, k, E, k - 4)
            sp.wait_ge(extra_ready, 1)
            n_extra = sp.value_load(extra_list[0:1, 2, 0:1], min_val=0, max_val=EXTRA)
            with sp.If(0 < n_extra):
                with sp.Fori(0, EXTRA) as i:
                    with sp.If(i < n_extra):
                        e = sp.value_load(extra_list[0:1, 0, bass.ds(i, 1)], min_val=0, max_val=E - 1)
                        for k in range(DOWN):
                            load_up(e, k, i + E, k)
                        for k in range(4):
                            load_down(e, k, i + E, k + DOWN)
            sp.wait_ge(y_all, 1)
            for t in range(NT):
                sp.dma_start(ytile[t], y_t[t]).then_inc(yt_in[t], 16)
                if t == 0:
                    sp.dma_start(g_fin, norm_final.partition_broadcast(P)).then_inc(gfin_in, 16)
            for t in range(NT):
                sp.wait_ge(o_ready, t + 1)
                sp.dma_start(out_t[t], ytile[t][:, D:2 * D]).then_inc(out_stored, 16)
            sp.wait_ge(out_stored, 16 * NT)

        @block.gpsimd
        def _(pool):
            g = nc.gpsimd

            def mean_rstd(r, t):
                pool.wait_ge(squares, NT * r + t + 1)
                g.tensor_scalar(sums[:, r, t:t + 1], sums[:, r, t:t + 1], 1.0 / D, EPS, ALU.mult, ALU.add)\
                 .then_inc(mean_ready, 1)
                pool.wait_ge(mean_ready, NT * r + t + 1)
                g.tensor_tensor(rstd[:, r, t:t + 1], sums[:, r, t:t + 1], half[:], ALU.pow).then_inc(rstd_ready, 1)

            g.memset(half[:], -0.5)
            g.memset(ident[:], 0.0).then_inc(id_step, 1)
            pool.wait_ge(id_step, 1)
            g.affine_select(out=ident[:], in_=ident[:], compare_op=ALU.not_equal, fill=1.0, base=0,
                            pattern=[[-1, P]], channel_multiplier=1).then_inc(id_step, 1)
            for t in range(NT):
                mean_rstd(0, t)
            g.memset(table0, 0).then_inc(tab_set, 1)
            pool.wait_ge(tab_set, 1)
            g.iota(table0[:, :, :, 1], [[0, BLOCKS], [0, E]], base=T * TOPE, channel_multiplier=1).then_inc(tab_set, 1)
            pool.wait_ge(tab_set, 2)
            pool.dma_start(table_init, table0.rearrange("s b e w -> s b (e w)")).then_inc(table_inited, 16)
            g.memset(diag[:], 0.0).then_inc(diag_step, 1)
            pool.wait_ge(diag_step, 1)
            g.affine_select(out=diag[:], in_=diag[:], compare_op=ALU.is_ge, fill=NEG, base=0,
                            pattern=[[-1, P]], channel_multiplier=1).then_inc(diag_step, 1)
            g.memset(ones[:], 1.0)
            g.memset(tri[:], 1.0).then_inc(tri_step, 1)
            pool.wait_ge(tri_step, 1)
            g.affine_select(out=tri[:], in_=tri[:], compare_op=ALU.is_gt, fill=0.0, base=0,
                            pattern=[[1, P]], channel_multiplier=-1)
            g.iota(e_row[:], [[1, E]], base=0, channel_multiplier=0, allow_small_or_imprecise_dtypes=True)
            g.iota(inv_n[:], [[0, NG], [1, PAD]], base=1, channel_multiplier=0,
                   allow_small_or_imprecise_dtypes=True)
            g.memset(expert_id[:], 0.0).then_inc(tri_step, 1)
            for r in range(2):
                pool.wait_ge(tri_step, 2 + r)
                g.affine_select(out=expert_id[:], in_=expert_id[:], compare_op=ALU.not_equal, fill=1.0,
                                base=-E * r, pattern=[[-1, E]], channel_multiplier=1).then_inc(tri_step, 1)
            g.memset(uT[:, :, 0:PAD], 0.0)
            g.memset(win[:, :, 0:PAD], 0.0).then_inc(const_ready, 1)
            pool.wait_ge(const_ready, 1)
            pool.wait_ge(inv_ready, NG)
            steps = 0
            for j, w in enumerate(WINDOWS):
                pool.wait_ge(evac_act, j + 1)
                src = uT[:, j, :]
                for lv in range(j + 1):
                    if steps:
                        pool.wait_ge(win_step, steps)
                    dst = win[:, lv % 2, :]
                    sh = 1 << lv
                    g.tensor_tensor(dst[:, PAD:], src[:, PAD:], src[:, PAD - sh:PAD + T - sh], ALU.add)\
                     .then_inc(win_step, 1)
                    steps += 1
                    src = dst
                pool.wait_ge(win_step, steps)
                g.tensor_scalar(src[:, 2 * PAD:], src[:, 2 * PAD:], 1.0 / w, None, ALU.mult)
                g.tensor_tensor(src[:, PAD:2 * PAD], src[:, PAD:2 * PAD], inv_n[:, j, :], ALU.mult).then_inc(win_step, 1)
                steps += 1
                pool.wait_ge(win_step, steps)
                g.tensor_tensor(uT[:, j, PAD:], src[:, PAD:], uT[:, j, PAD:], ALU.subtract).then_inc(pooled, 1)
                pool.wait_ge(pooled, j + 1)
            g.memset(payload[:], 0).then_inc(tab_set, 1)
            pool.wait_ge(tab_set, 3)
            pv = payload[:].rearrange("p (t k) w -> p t k w", t=NT)
            g.iota(pv[:, :, :, 0], [[P, NT], [0, TOPE]], base=0, channel_multiplier=1)
            g.iota(pv[:, :, :, 1], [[P * TOPE, NT], [1, TOPE]], base=0, channel_multiplier=TOPE)
            pool.wait_ge(half_squares, NT)
            g.tensor_scalar(half_sums[:], half_sums[:], EPS, None, ALU.add).then_inc(half_mean, 1)
            pool.wait_ge(half_mean, 1)
            for t in range(NT):
                pool.wait_ge(squares, NT + t + 1)
                g.tensor_tensor(sums[:, 1, t:t + 1], sums[:, 1, t:t + 1], half_sums[:, t:t + 1], ALU.add)\
                 .then_inc(mean_ready, 1)
                pool.wait_ge(mean_ready, NT + t + 1)
                g.tensor_tensor(rstd[:, 1, t:t + 1], sums[:, 1, t:t + 1], half[:], ALU.pow).then_inc(rstd_ready, 1)
            pool.wait_ge(out_mm, 2)
            g.iota(token_id[:], [[P, NT]], base=0, channel_multiplier=1, allow_small_or_imprecise_dtypes=True)
            g.iota(place_id[:], [[1, CAP]], base=0, channel_multiplier=0, allow_small_or_imprecise_dtypes=True)
            g.iota(limit[:], [[0, E], [CAP, BLOCKS - 1]], base=CAP, channel_multiplier=0,
                   allow_small_or_imprecise_dtypes=True)
            g.iota(code[:, 0, :], [[1, E], [0, BLOCKS - 1]], base=0, channel_multiplier=0,
                   allow_small_or_imprecise_dtypes=True)
            g.iota(code[:, 1, :], [[0, E], [1, BLOCKS - 1]], base=1, channel_multiplier=0,
                   allow_small_or_imprecise_dtypes=True)
            g.memset(picked[:], 1.0)
            g.iota(rank_id[:], [[0, 1]], base=1, channel_multiplier=1,
                   allow_small_or_imprecise_dtypes=True).then_inc(payload_set, 1)
            def table_rows(dst, e, blk):
                src = table_blk[:, bass.ds(blk, 1), bass.ds(e, 1), :]
                return pool.dma_start(dst[:].rearrange("s (b e w) -> s b e w", b=1, e=1), src)

            def hold():
                pool.sem_inc(pool_held, 1)

            def first_gather(e):
                pool.indirect_dma_start(xy[:], None, h2_dram,
                                        bass.IndirectOffsetOnAxis(start_tab[:, e:e + 1], 0)).then_inc(rows_in, 16)

            def gather(v, e, blk, load=True):
                if load:
                    table_rows(gather_tab, e, blk).then_inc(gtab_in, 16)
                pool.wait_ge(gtab_in, v * 16 - 16)
                hold()
                pool.indirect_dma_start(xy[:], None, h2_dram,
                                        bass.IndirectOffsetOnAxis(gather_tab[:, 0:1], 0)).then_inc(rows_in, 16)

            def choose_up(v, e):
                at_least(pool, up_bias_used, v)
                hold()
                g.tensor_copy(sel_up[:], expert_id[:, bass.ds(e, 1)].to_broadcast([2 * E, CAP]))\
                 .then_inc(sel_up_ready, 1)

            def choose_down(v, e):
                at_least(pool, down_bias_used, v)
                hold()
                g.tensor_copy(sel_down[:], expert_id[:, bass.ds(e, 1)].to_broadcast([2 * E, CAP]))\
                 .then_inc(sel_down_ready, 1)

            def scatter(v):
                pool.wait_ge(y_scaled, v + 1)
                hold()
                pool.indirect_dma_start(y_dram, bass.IndirectOffsetOnAxis(y_tab[:, 1:2], 0), xy[:], None)\
                    .then_inc(y_out, 16)
                pool.wait_ge(y_out, v * 16 + 16)

            def activation(v):
                pool.wait_ge(g_sig, v + 1)
                g.tensor_tensor(g_lin, g_lin, g_act, ALU.mult).then_inc(g_gated, 1)
                pool.wait_ge(g_gated, v + 1)
                pool.wait_ge(u_one, v + 1)
                g.tensor_tensor(g_act, g_lin, u_lin, ALU.mult).then_inc(act_ready, 1)

            pool.wait_ge(h2_stored, 16 * NT)
            pool.wait_ge(route, 3 * NT + 7)
            pool.wait_ge(start_ready, 1)
            first_gather(0)
            choose_up(0, 0)
            pool.wait_ge(table_inited, 16)
            pool.wait_ge(payload_ready, 1)
            for j in range(NT * TOPE):
                pool.indirect_dma_start(table_dram, bass.IndirectOffsetOnAxis(dest[:, j:j + 1], 0),
                                        payload[:, j, :], None).then_inc(table_done, 16)
            pool.wait_ge(rows_turned, 1)
            first_gather(1)
            choose_up(1, 1)
            choose_down(0, 0)
            activation(0)
            pool.wait_ge(table_done, 16 * NT * TOPE)
            table_rows(y_tab, 0, 0).then_inc(ytab_in, 16)
            pool.wait_ge(rows_turned, 2)
            gather(2, 2, 0)
            choose_up(2, 2)
            choose_down(1, 1)
            activation(1)

            def step(u, last=False):
                pool.wait_ge(rows_turned, u + 1)
                if not last:
                    table_rows(gather_tab, u + 1, 0).then_inc(gtab_in, 16)
                scatter(u - 2)
                table_rows(y_tab, u - 1, 0).then_inc(ytab_in, 16)
                if not last:
                    gather(u + 1, u + 1, 0, load=False)
                    choose_up(u + 1, u + 1)
                choose_down(u, u)
                activation(u)

            with pool.Fori(2, E - 1) as u:
                step(u)
            step(E - 1, last=True)
            scatter(E - 2)
            table_rows(y_tab, E - 1, 0).then_inc(ytab_in, 16)
            scatter(E - 1)
            pool.wait_ge(extra_ready, 1)
            n_extra = pool.value_load(extra_list[0:1, 2, 0:1], min_val=0, max_val=EXTRA)
            with pool.If(0 < n_extra):
                with pool.Fori(0, EXTRA) as i:
                    with pool.If(i < n_extra):
                        e = pool.value_load(extra_list[0:1, 0, bass.ds(i, 1)], min_val=0, max_val=E - 1)
                        b = pool.value_load(extra_list[0:1, 1, bass.ds(i, 1)], min_val=0, max_val=BLOCKS - 1)
                        gather(i + E, e, b)
                        choose_up(i + E, e)
                        choose_down(i + E, e)
                        table_rows(y_tab, e, b).then_inc(ytab_in, 16)
                        activation(i + E)
                        scatter(i + E)
            pool.sem_inc(y_all, 1)
            for t in range(NT):
                pool.wait_ge(yt_in[t], 16)
                g.tensor_tensor(ytile[t][:, 3 * D:], ytile[t][:, 2 * D:3 * D], ytile[t][:, 3 * D:], ALU.add)\
                 .then_inc(pair_sum, 1)
                if t >= 1:
                    mean_rstd(2, t - 1)
            mean_rstd(2, NT - 1)

        @block.scalar
        def _(act):
            s = nc.scalar

            def hi_part(i):
                g = i // 4
                act.wait_ge(wgroup_in[g % 2], 16 * (g // 2 + 1))
                if g in (7, 8):
                    act.wait_ge(pu_in[g - 7], 16)
                if i >= 4:
                    act.wait_ge(piece_done, i - 3)
                s.activation(split_piece(whi, i), raw_piece(i), ACT.Copy).then_inc(hi_done, 1)

            def square(r, t, src, dst):
                s.activation(dst, src, ACT.Square, accum_out=sums[:, r, t:t + 1]).then_inc(squares, 1)

            for t in range(NT):
                act.wait_ge(x_in[t], 16)
                square(0, t, xN[:, t, :], hN[:, t, :])
            for i in range(3):
                hi_part(i)
            act.wait_ge(small_in, 112)
            for c in range(KC):
                act.wait_ge(h_turned, c + 1)
                s.activation(xTh[:, c, :], ps[:, 6 + c % 2, :], ACT.Copy, scale=g_mix[:, c:c + 1]).then_inc(xT_hi, 1)

            def relus(t, h):
                n = 2 * (t - 1) + h
                act.wait_ge(idx_done, n + 1)
                if n:
                    act.wait_ge(score_step, 4 * n)
                s.activation(prob[:, 0, :, 0:P * (t + 1)], ps[:, 2:6, 0:P * (t + 1)], ACT.Relu).then_inc(relu_done, 1)

            for i in range(N_PROJ):
                hi_part(i + 3)
                act.wait_ge(piece_done, i + 1)
                if U_PIECE <= i < G_PIECE:
                    s.activation(uT[:, i - U_PIECE, PAD:], ps[:, i % 2, :], ACT.Copy).then_inc(evac_act, 1)
                elif i >= G_PIECE:
                    s.activation(gates[:, i - G_PIECE, :], ps[:, i % 2, :], ACT.Sigmoid).then_inc(evac_act, 1)
                if 9 <= i < 9 + 2 * (NT - 1):
                    relus(1 + (i - 9) // 2, (i - 9) % 2)
            for j in range(NG):
                act.wait_ge(pool_mixed, j + 1)
                s.activation(xTh[:, 4 + j, :], ps[:, j % 2, :], ACT.Copy, scale=p_scale[:, j:j + 1]).then_inc(pool_hi, 1)

            def exps(a):
                t, g = attn[a]
                act.wait_ge(nmax_ready, a + 1)
                for j in range(4):
                    last = s.activation(prob[:, a % 2, j, 0:P * (t + 1)], prob[:, a % 2, j, 0:P * (t + 1)], ACT.Exp,
                                        bias=nmax[:, a % 2, j:j + 1], accum_out=psumx[:, t % 2, 4 * g + j:4 * g + j + 1])
                last.then_inc(exp_done, 1)

            def y_high(t):
                act.wait_ge(y_turned, t + 1)
                s.activation(xTh[:, 0:4, t * P:(t + 1) * P], ps[:, t % 2, :].rearrange("p (c n) -> p c n", c=4),
                             ACT.Copy).then_inc(y_hi, 1)

            exps(0)
            for a, (t, g) in enumerate(attn):
                for n in range(blocks_to[a], blocks_to[a + 1]):
                    if n % 2 == 0:
                        act.wait_ge(p_turned, n + 1)
                        if n >= 2:
                            act.wait_ge(pv_done, n - 1)
                        s.activation(pT[:, 0, :], ps[:, 6, :], ACT.Copy).then_inc(pT_even, 1)
                if a + 1 < len(attn):
                    exps(a + 1)
                if g == 0 and t >= 1:
                    y_high(t - 1)
            y_high(NT - 1)
            for m in range(N_UP):
                hi_part(N_PROJ + m + 3)
                act.wait_ge(mix_sum, m + 1)
                s.activation(mTh[:, m, :], t_at[:], ACT.Copy).then_inc(mT_hi, 1)
            for i in range(N_PROJ + N_UP + 3, N_PIECES):
                hi_part(i)
            act.wait_ge(x2_left, 1)
            for t in range(NT):
                if t:
                    act.wait_ge(half_squares, t)
                s.activation(t_at[:], X[:, t, 0:T], ACT.Square, scale=D ** -0.5, accum_out=half_sums[:, t:t + 1])\
                 .then_inc(half_squares, 1)
            for c in range(0, KC // 2, 2):
                act.wait_ge(h2_turned, c + 1)
                s.activation(h2T(c), ps[:, turn_bank(c), :], ACT.Copy).then_inc(h2T_act, 1)
            act.wait_ge(half_squares, NT)
            for t in range(NT):
                act.wait_ge(x2_right, t + 1)
                if t:
                    act.wait_ge(squares, NT + t)
                s.activation(t_at[:], X[:, t, T:D], ACT.Square, scale=D ** -0.5, accum_out=sums[:, 1, t:t + 1])\
                 .then_inc(squares, 1)
            for c in range(KC // 2, KC, 2):
                act.wait_ge(h2_turned, c + 1)
                s.activation(h2T(c), ps[:, turn_bank(c), :], ACT.Copy).then_inc(h2T_act, 1)
            act.wait_ge(router_mm, 1)
            s.activation(t_po[0:E, :], ps[0:E, 4, :], ACT.Copy).then_inc(logits_out, 1)
            act.wait_ge(route, 3 * NT + 2)
            for t in range(NT):
                s.activation(ex[:, t, :], v8[:, t, 0:TOPE], ACT.Exp, bias=nv0[:, t:t + 1],
                             accum_out=exs[:, t:t + 1]).then_inc(exp_gate, 1)

            act.wait_ge(bias_in, 64)
            s.activation(bias[:], bias_raw, ACT.Copy).then_inc(bias_hi, 1)

            def ehi(u, off):
                act.wait_ge(raw_in[slot_of(off)], u * 16 + 16 * (off // STEP + 1))
                at_least(act, chunk_used, u * STEP + (off - SPLIT + 1))
                s.activation(hi[:, half_of(off), :], raw[:, slot_of(off), :], ACT.Copy).then_inc(ehi_done, 1)

            def xe_high(v):
                at_least(act, gu_done, v)
                act.wait_ge(rows_turned, v + 1)
                s.activation(xeh[:].rearrange("p (b c) n -> p b (c n)", b=2), ps[:, 6:8, 0:4 * CAP], ACT.Copy)\
                 .then_inc(xe_hi, 1)

            def sigmoid(v):
                act.wait_ge(g_clip, v + 1)
                s.activation(g_act, g_lin, ACT.Sigmoid, scale=ALPHA).then_inc(g_sig, 1)

            def plus_one(v):
                act.wait_ge(u_clip, v + 1)
                s.activation(u_lin, u_lin, ACT.Copy, bias=1.0).then_inc(u_one, 1)

            def aT_high(v):
                act.wait_ge(act_turned, v + 1)
                s.activation(aTh[:].rearrange("p (b c) n -> p b (c n)", b=2), ps[:, 6:8, 0:4 * CAP], ACT.Copy)\
                 .then_inc(aT_hi, 1)

            def scale_y(v):
                act.wait_ge(down_done, v + 1)
                act.wait_ge(ytab_in, v * 16 + 16)
                s.activation(xy[:], ps[0:CAP, 4:6, :].rearrange("p b n -> p (b n)"), ACT.Copy,
                             scale=y_tab[:, 2:3].bitcast(F32)).then_inc(y_scaled, 1)

            def end_of_step(u, off, more=True):
                for k in (8, 9, 10):
                    ehi(u, off + k)
                sigmoid(u)
                ehi(u, off + 11)
                plus_one(u)
                if more:
                    xe_high(u + 1)

            xe_high(0)
            act.wait_ge(h2_stored, 16 * NT)
            for k in range(DOWN):
                ehi(0, k)
            sigmoid(0)
            plus_one(0)
            xe_high(1)

            def step(u, first=False, last=False):
                ehi(u, -4)
                ehi(u, -3)
                if not first:
                    act.wait_ge(rows_turned, u + 1)
                    scale_y(u - 2)
                ehi(u, -2)
                ehi(u, -1)
                aT_high(u - 1)
                for k in range(4, DOWN):
                    ehi(u, k - 4)
                end_of_step(u, -4, more=not last)

            step(1, first=True)
            with act.Fori(2, E - 1) as u:
                step(u)
            step(E - 1, last=True)
            for k in range(SPLIT):
                ehi(E, k - 4)
                if k == 1:
                    scale_y(E - 2)
            aT_high(E - 1)
            ehi(E, SPLIT - 4)
            scale_y(E - 1)
            act.wait_ge(extra_ready, 1)
            n_extra = act.value_load(extra_list[0:1, 2, 0:1], min_val=0, max_val=EXTRA)
            with act.If(0 < n_extra):
                with act.Fori(0, EXTRA) as i:
                    with act.If(i < n_extra):
                        v = i + E
                        xe_high(v)
                        for k in range(DOWN):
                            ehi(v, k)
                        sigmoid(v)
                        plus_one(v)
                        for k in range(DOWN, STEP - 1):
                            ehi(v, k)
                        aT_high(v)
                        ehi(v, STEP - 1)
                        scale_y(v)
            for t in range(NT):
                act.wait_ge(comb, 3 * t + 3)
                square(2, t, X[:, t, :], ytile[t][:, 0:D])

        @block.vector
        def _(dve):
            v_ = nc.vector

            def lo_part(i):
                dve.wait_ge(hi_done, i + 1)
                v_.tensor_tensor(split_piece(wlo, i), raw_piece(i), split_piece(whi, i).bitcast(F32), ALU.subtract)\
                  .then_inc(lo_done, 1)

            for t in range(NT):
                dve.wait_ge(rstd_ready, t + 1)
                v_.tensor_scalar(hN[:, t, :], xN[:, t, :], rstd[:, 0, t:t + 1], None, ALU.mult).then_inc(h_ready, 1)
            for i in range(3):
                lo_part(i)
            dve.wait_ge(small_in, 112)
            for c in range(KC):
                dve.wait_ge(xT_hi, c + 1)
                v_.scalar_tensor_tensor(xTl[:, c, :], ps[:, 6 + c % 2, :], g_mix[:, c:c + 1], xTh[:, c, :].bitcast(F32),
                                        ALU.mult, ALU.subtract).then_inc(xT_lo, 1)
            v_.tensor_tensor(wr[:], wr[:], g_ffc[:].unsqueeze(2).to_broadcast([P, KC, E]), ALU.mult)\
              .then_inc(wr_scaled, 1)
            dve.wait_ge(const_ready, 1)
            for j, w in enumerate(WINDOWS):
                v_.tensor_scalar(inv_n[:, j, :], inv_n[:, j, :], float(w), None, ALU.min).then_inc(inv_step, 1)
                dve.wait_ge(inv_step, j + 1)
                v_.reciprocal(inv_n[:, j, :], inv_n[:, j, :]).then_inc(inv_ready, 1)

            def evacuate(i):
                dve.wait_ge(piece_done, i + 1)
                src = ps[:, i % 2, :]
                if i < Q_PIECES:
                    last = v_.tensor_copy(qT[:, i, :], src)
                elif i == 4:
                    v_.tensor_copy(kT[0:DH, :], src[0:DH, :])
                    v_.tensor_copy(kT[DH:2 * DH, :], src[0:DH, :])
                    last = v_.tensor_copy(vT[DH:2 * DH, :], src[DH:2 * DH, :])
                elif i < 7:
                    last = v_.tensor_copy(iqT[:, i - 5, :], src)
                else:
                    for r in range(4):
                        v_.tensor_copy(ikT[r * DI:(r + 1) * DI, :], src[0:DI, :])
                    last = v_.tensor_copy(vT[DI:DI + NI, :], src[DI:DI + NI, :])
                last.then_inc(evac_dve, 1)

            def add_heads(t, h):
                n = 2 * (t - 1) + h
                nk = P * (t + 1)
                dve.wait_ge(relu_done, n + 1)
                if n:
                    dve.wait_ge(score_step, 4 * n)
                sc = score[:, t - 1, 0:nk]
                for j in range(4):
                    w = iw[:, t, 4 * h + j:4 * h + j + 1]
                    if h == 0 and j == 0:
                        v_.tensor_scalar(sc, prob[:, 0, j, 0:nk], w, None, ALU.mult).then_inc(score_step, 1)
                    else:
                        dve.wait_ge(score_step, 4 * n + j)
                        v_.scalar_tensor_tensor(sc, prob[:, 0, j, 0:nk], w, sc, ALU.mult, ALU.add)\
                          .then_inc(score_step, 1)
                if h == 1:
                    dve.wait_ge(score_step, 4 * n + 4)
                    v_.tensor_tensor(sc[:, t * P:], sc[:, t * P:], diag[:], ALU.add).then_inc(diag_added, 1)
                    dve.wait_ge(diag_added, t)

            rounds_done = [0]

            def topk(t, r0, r1):
                sc = score[:, t - 1, 0:P * (t + 1)]
                for r in range(r0, r1):
                    n = 2 * (NROUND * (t - 1) + r)
                    if n:
                        dve.wait_ge(topk_step, n)
                    v_.max(top8[:], sc).then_inc(topk_step, 1)
                    dve.wait_ge(topk_step, n + 1)
                    v_.match_replace(sc, top8[:], sc, TAKEN).then_inc(topk_step, 1)
                if r1 == NROUND:
                    dve.wait_ge(topk_step, 2 * NROUND * t)
                    v_.tensor_scalar(sc, sc, TAKEN / 2, NEG, ALU.is_gt, ALU.mult).then_inc(mask_out, 1)

            dve.wait_ge(diag_step, 2)
            for i in range(N_PROJ):
                lo_part(i + 3)
                if i < U_PIECE:
                    evacuate(i)
                if i == U_PIECE:
                    dve.wait_ge(v_turned, 1)
                    v_.tensor_copy(v_sb[:], ps[:, 6, 0:NT * DH].rearrange("p (t d) -> p t d", t=NT))
                    v_.tensor_scalar(iw[:], ps[:, 6, 256:256 + NT * NI].rearrange("p (t d) -> p t d", t=NT),
                                     (NI ** -0.5) * (DI ** -0.5), None, ALU.mult).then_inc(v_ready, 1)
                    dve.wait_ge(v_ready, 1)
                if 10 <= i < 10 + 2 * (NT - 1):
                    add_heads(1 + (i - 10) // 2, (i - 10) % 2)
                if i in (13, 15):
                    topk(1, 8 * (i == 15), 8 + 8 * (i == 15))
                if 16 <= i < 20:
                    topk(2, 4 * (i - 16), 4 * (i - 15))
                if 20 <= i < 25:
                    topk(3, 3 * (i - 20), 3 * (i - 19) + (i == 24))
            for j in range(NG):
                dve.wait_ge(pool_hi, j + 1)
                v_.scalar_tensor_tensor(xTl[:, 4 + j, :], ps[:, j % 2, :], p_scale[:, j:j + 1],
                                        xTh[:, 4 + j, :].bitcast(F32), ALU.mult, ALU.subtract).then_inc(pool_lo, 1)

            def mask_logits(a):
                t, g = attn[a]
                nk = P * (t + 1)
                dve.wait_ge(logits_done, a + 1)
                if a >= 2:
                    dve.wait_ge(p_turned, blocks_to[a - 1])
                if a == 0:
                    dve.wait_ge(mask_out, NT - 1)
                if a == 1:
                    dve.wait_ge(table_inited, 16)
                pr = prob[:, a % 2, :, 0:nk]
                v_.scalar_tensor_tensor(pr, ps[:, 2:6, 0:nk], DH ** -0.5, selected(t), ALU.mult, ALU.add)\
                  .then_inc(masked, 1)
                dve.wait_ge(masked, a + 1)
                v_.tensor_reduce(nmax[:, a % 2, :], pr, AX_X, ALU.max).then_inc(max_found, 1)
                dve.wait_ge(max_found, a + 1)
                v_.tensor_scalar(nmax[:, a % 2, :], nmax[:, a % 2, :], -1.0, None, ALU.mult).then_inc(nmax_ready, 1)

            def y_low(t):
                dve.wait_ge(y_hi, t + 1)
                v_.tensor_tensor(xTl[:, 0:4, t * P:(t + 1) * P], ps[:, t % 2, :].rearrange("p (c n) -> p c n", c=4),
                                 xTh[:, 0:4, t * P:(t + 1) * P].bitcast(F32), ALU.subtract).then_inc(y_lo, 1)

            mask_logits(0)
            for a, (t, g) in enumerate(attn):
                if a + 1 < len(attn):
                    mask_logits(a + 1)
                for n in range(blocks_to[a], blocks_to[a + 1]):
                    if n % 2:
                        dve.wait_ge(p_turned, n + 1)
                        if n >= 2:
                            dve.wait_ge(pv_done, n - 1)
                        v_.tensor_copy(pT[:, 1, :], ps[:, 7, :]).then_inc(pT_odd, 1)
                if g == 0 and t >= 1:
                    y_low(t - 1)
                if g == 1:
                    dve.wait_ge(exp_done, a + 1)
                    v_.reciprocal(pinv[:], psumx[:, t % 2, :]).then_inc(pinv_ready, 1)
                    dve.wait_ge(pinv_ready, t + 1)
                    dve.wait_ge(pv_done, blocks_to[a + 1])
                    if t:
                        dve.wait_ge(y_turned, t)
                    v_.tensor_tensor(yN[:].rearrange("p (h d) -> p h d", h=NH),
                                     ps[:, t % 2, :].rearrange("p (h d) -> p h d", h=NH),
                                     pinv[:].unsqueeze(2).to_broadcast([P, NH, DH]), ALU.mult).then_inc(y_norm, 1)
            y_low(NT - 1)
            for m in range(N_UP):
                lo_part(N_PROJ + m + 3)
                dve.wait_ge(piece_done, N_PROJ + m + 1)
                if m:
                    dve.wait_ge(mT_lo, m)
                b = 2 * (m % 2)
                v_.tensor_tensor(t_at[:], ps[:, b, :], gates[:, m, :], ALU.mult).then_inc(gated_a, 1)
                v_.tensor_tensor(t_po[:], ps[:, b + 1, :], gates[:, KC + m, :], ALU.mult).then_inc(gated_p, 1)
                dve.wait_ge(gated_a, m + 1)
                dve.wait_ge(gated_p, m + 1)
                v_.tensor_tensor(t_at[:], t_at[:], t_po[:], ALU.add).then_inc(mix_sum, 1)
                dve.wait_ge(mix_sum, m + 1)
                dve.wait_ge(mT_hi, m + 1)
                v_.tensor_tensor(mTl[:, m, :], t_at[:], mTh[:, m, :].bitcast(F32), ALU.subtract).then_inc(mT_lo, 1)
            for i in range(N_PROJ + N_UP + 3, N_PIECES):
                lo_part(i)
            dve.wait_ge(x_again, 16 * NT)
            dve.wait_ge(out_mm, 1)
            v_.tensor_tensor(X[:, :, 0:T], X[:, :, 0:T], ps[:, 4:8, :], ALU.add).then_inc(x2_left, 1)

            def turned_out(c):
                dve.wait_ge(h2_turned, c + 1)
                v_.tensor_copy(h2T(c), ps[:, turn_bank(c), :]).then_inc(h2T_dve, 1)

            turned_out(1)
            turned_out(3)
            dve.wait_ge(out_mm, 2)
            for t in range(NT):
                v_.tensor_tensor(X[:, t, T:D], X[:, t, T:D], ps[:, t, :], ALU.add).then_inc(x2_right, 1)
            turned_out(5)
            turned_out(7)
            dve.wait_ge(x2_left, 1)
            dve.wait_ge(x2_right, NT)
            for t in range(NT):
                dve.wait_ge(rstd_ready, NT + t + 1)
                v_.scalar_tensor_tensor(h2N[:, t, :], X[:, t, :], rstd[:, 1, t:t + 1], g_ffn[:], ALU.mult, ALU.mult)\
                  .then_inc(h2_ready, 1)
            for t in range(NT):
                dve.wait_ge(logits_turned, 1)
                v_.scalar_tensor_tensor(lg[:, t, :], ps[:, 1, t * E:(t + 1) * E], rstd[:, 1, t:t + 1], br[:],
                                        ALU.mult, ALU.add).then_inc(route, 1)
            for t in range(NT):
                dve.wait_ge(route, NT + 2 * t if t else NT)
                v_.max(v8[:, t, :], lg[:, t, :]).then_inc(route, 1)
                dve.wait_ge(route, NT + 2 * t + 1)
                v_.max_index(i8[:, t, :], v8[:, t, :], lg[:, t, :]).then_inc(route, 1)
            dve.wait_ge(route, 3 * NT)
            v_.tensor_scalar(nv0[:], v8[:, :, 0], -1.0, None, ALU.mult).then_inc(route, 1)
            v_.tensor_copy(i4[:].rearrange("p (t k) -> p t k", t=NT), i8[:, :, 0:TOPE]).then_inc(route, 1)
            dve.wait_ge(route, 3 * NT + 2)
            v_.tensor_tensor(hot[:], e_row[:].unsqueeze(1).to_broadcast([P, NT * TOPE, E]),
                             i4[:].unsqueeze(2).to_broadcast([P, NT * TOPE, E]), ALU.is_equal).then_inc(route, 1)
            dve.wait_ge(route, 3 * NT + 3)
            v_.tensor_reduce(mask[:], hot[:].rearrange("p (t k) e -> p t e k", t=NT), AX_X, ALU.max)\
              .then_inc(mask_ready, 1)
            dve.wait_ge(exp_gate, NT)
            v_.reciprocal(exr[:], exs[:]).then_inc(route, 1)
            dve.wait_ge(route, 3 * NT + 4)
            dve.wait_ge(payload_set, 1)
            v_.tensor_tensor(payload[:, :, 2].bitcast(F32).rearrange("p (t k) -> p t k", t=NT), ex[:],
                             exr[:].unsqueeze(2).to_broadcast([P, NT, TOPE]), ALU.mult).then_inc(route, 1)
            v_.tensor_tensor(start_tok[:], token_id[:].unsqueeze(1).to_broadcast([P, 2, NT]),
                             mask[:, :, 0:2].rearrange("p t e -> p e t"), ALU.mult).then_inc(start_step, 1)
            dve.wait_ge(pos_mm, 1)
            for e in range(2):
                v_.tensor_tensor(start_sel[:, e],
                                 ps[:, 7, 0:NT * E].rearrange("p (t e) -> p t e", t=NT)[:, :, e:e + 1]
                                 .to_broadcast([P, NT, CAP]),
                                 place_id[:].unsqueeze(1).to_broadcast([P, NT, CAP]), ALU.is_equal)\
                  .then_inc(start_step, 1)
            v_.scalar_tensor_tensor(dpos[:], ps[:, 7, 0:NT * E].rearrange("p (t e) -> p t e", t=NT), float(E),
                                    e_row[:].unsqueeze(1).to_broadcast([P, NT, E]), ALU.mult, ALU.add)
            v_.tensor_copy(cnt[:], ps[:, 7, NT * E:NT * E + E]).then_inc(route, 1)
            dve.wait_ge(route, 3 * NT + 6)
            v_.tensor_tensor(prod[:].rearrange("p (t k) e -> p t k e", t=NT),
                             hot[:].rearrange("p (t k) e -> p t k e", t=NT),
                             dpos[:].unsqueeze(2).to_broadcast([P, NT, TOPE, E]), ALU.mult).then_inc(route, 1)
            dve.wait_ge(start_mm, 1)
            v_.tensor_copy(start_tab[:], ps[0:CAP, 5, 0:2]).then_inc(start_ready, 1)
            dve.wait_ge(route, 3 * NT + 7)
            v_.tensor_reduce(dest_f[:], prod[:], AX_X, ALU.add).then_inc(route, 1)
            dve.wait_ge(route, 3 * NT + 8)
            v_.tensor_copy(dest[:], dest_f[:]).then_inc(payload_ready, 1)
            v_.tensor_tensor(over[:].rearrange("p (e b) -> p e b", e=E),
                             cnt[:].unsqueeze(2).to_broadcast([P, E, BLOCKS - 1]),
                             limit[:].rearrange("p (e b) -> p e b", e=E), ALU.is_gt).then_inc(extra_step, 1)
            dve.wait_ge(extra_step, 1)
            v_.tensor_tensor_scan(rank[:], picked[:], over[:], 0.0, ALU.mult, ALU.add).then_inc(extra_step, 1)
            dve.wait_ge(extra_step, 2)
            v_.scalar_tensor_tensor(picked[:], rank[:], rank_id[:, 0:1], over[:], ALU.is_equal, ALU.mult)
            v_.tensor_copy(found[:, 2:3], rank[:, CAND - 1:CAND]).then_inc(extra_step, 1)
            dve.wait_ge(extra_step, 3)
            v_.tensor_tensor(pick2[:], picked[:].unsqueeze(1).to_broadcast([P, 2, CAND]), code[:], ALU.mult)\
              .then_inc(extra_step, 1)
            dve.wait_ge(extra_step, 4)
            v_.tensor_reduce(found[:, 0:2], pick2[:], AX_X, ALU.add).then_inc(extra_fill, 1)
            dve.wait_ge(extra_mm, 1)
            v_.tensor_copy(extra_list[:], ps[0:1, 4, 0:3 * P].rearrange("p (a n) -> p a n", a=3)[:, :, 0:32])\
              .then_inc(extra_ready, 1)
            dve.wait_ge(bias_hi, 1)
            v_.tensor_tensor(bias[E:2 * E, :], bias_raw[E:2 * E, :], bias[E:2 * E, :].bitcast(F32), ALU.subtract)\
              .then_inc(bias_lo, 1)

            def elo(u, off):
                dve.wait_ge(ehi_done, u * STEP + (off + 1))
                v_.tensor_tensor(lo[:, half_of(off), :], raw[:, slot_of(off), :], hi[:, half_of(off), :].bitcast(F32),
                                 ALU.subtract).then_inc(elo_done, 1)

            def xe_low(v):
                dve.wait_ge(xe_hi, v + 1)
                v_.tensor_tensor(xel[:].rearrange("p (b c) n -> p b (c n)", b=2), ps[:, 6:8, 0:4 * CAP],
                                 xeh[:].rearrange("p (b c) n -> p b (c n)", b=2).bitcast(F32), ALU.subtract)\
                  .then_inc(xe_lo, 1)

            pairs = ps[0:CAP, 0:4, :].rearrange("p b (n two) -> p (b n) two", two=2)

            def clip_g(v):
                dve.wait_ge(gu_done, v + 1)
                at_least(dve, act_turned, v)
                v_.tensor_scalar(g_lin, pairs[:, :, 0], LIMIT, None, ALU.min).then_inc(g_clip, 1)

            def clip_u(v):
                v_.tensor_scalar(u_lin, pairs[:, :, 1], LIMIT, -LIMIT, ALU.min, ALU.max).then_inc(u_clip, 1)

            def aT_low(v):
                dve.wait_ge(aT_hi, v + 1)
                v_.tensor_tensor(aTl[:].rearrange("p (b c) n -> p b (c n)", b=2), ps[:, 6:8, 0:4 * CAP],
                                 aTh[:].rearrange("p (b c) n -> p b (c n)", b=2).bitcast(F32), ALU.subtract)\
                  .then_inc(aT_lo, 1)

            xe_low(0)
            for k in range(DOWN):
                elo(0, k)
            clip_g(0)
            clip_u(0)
            xe_low(1)

            def step(u, last=False):
                for k in range(4):
                    elo(u, k - 4)
                aT_low(u - 1)
                for k in range(4, 10):
                    elo(u, k - 4)
                clip_g(u)
                elo(u, 6)
                clip_u(u)
                elo(u, 7)
                if not last:
                    xe_low(u + 1)

            step(1)
            with dve.Fori(2, E - 1) as u:
                step(u)
            step(E - 1, last=True)
            for k in range(SPLIT):
                elo(E, k - 4)
            aT_low(E - 1)
            elo(E, SPLIT - 4)
            n_extra = dve.value_load(extra_list[0:1, 2, 0:1], min_val=0, max_val=EXTRA)
            with dve.If(0 < n_extra):
                with dve.Fori(0, EXTRA) as i:
                    with dve.If(i < n_extra):
                        v = i + E
                        xe_low(v)
                        for k in range(DOWN):
                            elo(v, k)
                        clip_g(v)
                        clip_u(v)
                        for k in range(DOWN, STEP - 1):
                            elo(v, k)
                        aT_low(v)
                        elo(v, STEP - 1)
            def finish(t):
                dve.wait_ge(rstd_ready, 2 * NT + t + 1)
                dve.wait_ge(gfin_in, 16)
                v_.scalar_tensor_tensor(ytile[t][:, D:2 * D], X[:, t, :], rstd[:, 2, t:t + 1], g_fin,
                                        ALU.mult, ALU.mult).then_inc(o_ready, 1)

            for t in range(NT):
                yt = ytile[t]
                dve.wait_ge(yt_in[t], 16)
                v_.tensor_tensor(yt[:, 0:D], yt[:, 0:D], yt[:, D:2 * D], ALU.add).then_inc(comb, 1)
                dve.wait_ge(comb, 3 * t + 1)
                v_.tensor_tensor(X[:, t, :], X[:, t, :], yt[:, 0:D], ALU.add).then_inc(comb, 1)
                dve.wait_ge(comb, 3 * t + 2)
                dve.wait_ge(pair_sum, t + 1)
                v_.tensor_tensor(X[:, t, :], X[:, t, :], yt[:, 3 * D:], ALU.add).then_inc(comb, 1)
                dve.wait_ge(comb, 3 * t + 3)
                if t >= 1:
                    finish(t - 1)
            finish(NT - 1)

        @block.tensor
        def _(pe):
            m_ = nc.tensor.matmul

            def three(o, ah, al, bh, bl, start, stop):
                m_(o, ah, bh, start=start, stop=False)
                m_(o, ah, bl, start=False, stop=False)
                return m_(o, al, bh, start=False, stop=stop)

            pe.wait_ge(id_step, 2)
            for c in range(KC):
                if c >= 2:
                    pe.wait_ge(xT_lo, c - 1)
                for t in range(NT):
                    if c == 0:
                        pe.wait_ge(h_ready, t + 1)
                    last = nc.tensor.transpose(ps[:, 6 + c % 2, t * P:(t + 1) * P], hN[:, t, c * P:(c + 1) * P], ident[:])
                last.then_inc(h_turned, 1)

            def turn_values():
                pe.wait_ge(evac_dve, 8)
                for t in range(NT):
                    nc.tensor.transpose(ps[:, 6, t * DH:(t + 1) * DH], vT[DH:2 * DH, t * P:(t + 1) * P],
                                        ident[DH:2 * DH, DH:2 * DH])
                for t in range(NT):
                    last = nc.tensor.transpose(ps[:, 6, 256 + t * NI:256 + (t + 1) * NI],
                                               vT[DI:DI + NI, t * P:(t + 1) * P], ident[DI:DI + NI, DI:DI + NI])
                last.then_inc(v_turned, 1)

            def index_products(t, h):
                n = 2 * (t - 1) + h
                if n:
                    pe.wait_ge(relu_done, n)
                nk = P * (t + 1)
                for j in range(4):
                    r = slice(j * DI, (j + 1) * DI)
                    last = m_(ps[:, 2 + j, 0:nk], iqT[r, h, t * P:(t + 1) * P], ikT[r, 0:nk], start=True, stop=True)
                last.then_inc(idx_done, 1)

            pe.wait_ge(xT_lo, KC)
            for i in range(N_PROJ):
                pe.wait_ge(lo_done, i + 1)
                if 2 <= i < U_PIECE + 2:
                    pe.wait_ge(evac_dve, i - 1)
                if i >= U_PIECE + 2:
                    pe.wait_ge(evac_act, i - U_PIECE - 1)
                wh, wl = split_piece(whi, i), split_piece(wlo, i)
                for c in range(KC):
                    last = three(ps[:, i % 2, :], wh[:, c, :], wl[:, c, :], xTh[:, c, :], xTl[:, c, :],
                                 c == 0, c == KC - 1)
                last.then_inc(piece_done, 1)
                if i == U_PIECE:
                    turn_values()
                if 9 <= i < 9 + 2 * (NT - 1):
                    index_products(1 + (i - 9) // 2, (i - 9) % 2)
            pe.wait_ge(evac_act, N_PROJ - U_PIECE)
            for j in range(NG):
                pe.wait_ge(pooled, j + 1)
                if j >= 2:
                    pe.wait_ge(pool_lo, j - 1)
                m_(ps[:, j % 2, :], wp[:, j, :], uT[:, j, PAD:], start=True, stop=True).then_inc(pool_mixed, 1)

            def logits(a):
                t, g = attn[a]
                nk = P * (t + 1)
                if a:
                    pe.wait_ge(masked, a)
                for j in range(4):
                    h = 4 * g + j
                    r = slice(DH * (h % 2), DH * (h % 2) + DH)
                    last = m_(ps[:, 2 + j, 0:nk], qT[r, h // 2, t * P:(t + 1) * P], kT[r, 0:nk], start=True, stop=True)
                last.then_inc(logits_done, 1)

            def weigh(a, n):
                t, g = attn[a]
                kb = n - blocks_to[a]
                pT_evacuated(pe, n)
                for j in range(4):
                    h = 4 * g + j
                    last = m_(ps[:, t % 2, h * DH:(h + 1) * DH], pT[:, n % 2, j * P:(j + 1) * P], v_sb[:, kb, :],
                              start=(g == 0 and kb == 0 and j == 0), stop=(kb == t), skip_group_check=True)
                last.then_inc(pv_done, 1)

            def turn_y(t):
                pe.wait_ge(y_norm, t + 1)
                for c in range(4):
                    last = nc.tensor.transpose(ps[:, t % 2, c * P:(c + 1) * P], yN[:, c * P:(c + 1) * P], ident[:])
                last.then_inc(y_turned, 1)

            logits(0)
            pe.wait_ge(pool_lo, NG)
            for a, (t, g) in enumerate(attn):
                if a + 1 < len(attn):
                    logits(a + 1)
                pe.wait_ge(exp_done, a + 1)
                if g == 0 and t >= 2:
                    pe.wait_ge(y_lo, t - 1)
                for n in range(blocks_to[a], blocks_to[a + 1]):
                    if n >= 2:
                        pT_evacuated(pe, n - 2)
                    kb = n - blocks_to[a]
                    for j in range(4):
                        last = nc.tensor.transpose(ps[:, 6 + n % 2, j * P:(j + 1) * P],
                                                   prob[:, a % 2, j, kb * P:(kb + 1) * P], ident[:])
                    last.then_inc(p_turned, 1)
                    if n > blocks_to[a]:
                        weigh(a, n - 1)
                weigh(a, blocks_to[a + 1] - 1)
                if g == 0 and t >= 1:
                    turn_y(t - 1)
            turn_y(NT - 1)
            pe.wait_ge(y_lo, NT)
            for m in range(N_UP):
                i = N_PROJ + m
                pe.wait_ge(lo_done, i + 1)
                if m >= 2:
                    pe.wait_ge(gated_p, m - 1)
                wh, wl = split_piece(whi, i), split_piece(wlo, i)
                for c in range(KC):
                    last = three(ps[:, 2 * (m % 2) + c // 4, :], wh[:, c, :], wl[:, c, :], xTh[:, c, :], xTl[:, c, :],
                                 c % 4 == 0, c % 4 == 3)
                last.then_inc(piece_done, 1)
            pe.wait_ge(mT_lo, N_UP)

            def turn_x2(c, t):
                return nc.tensor.transpose(ps[:, turn_bank(c), t * P:(t + 1) * P], X[:, t, c * P:(c + 1) * P], ident[:])

            def route_chunk(c):
                pe.wait_ge(h2T_dve if c % 2 else h2T_act, c // 2 + 1)
                return m_(ps[0:E, 4, :], wr[:, c, :], h2T(c), start=(c == 0), stop=(c == KC - 1))

            for n in range(2):
                for j in range(4):
                    i = N_PROJ + N_UP + 4 * n + j
                    pe.wait_ge(lo_done, i + 1)
                    wh, wl = split_piece(whi, i), split_piece(wlo, i)
                    for cc in range(2):
                        c = 2 * j + cc
                        for t in range(NT):
                            r = slice(t * P, (t + 1) * P)
                            last = three(ps[:, 4 - 4 * n + t, :], mTh[:, c, r], mTl[:, c, r], wh[:, cc, :], wl[:, cc, :],
                                         c == 0, c == KC - 1)
                    last.then_inc(piece_done, 1)
                    if n == 1 and j == 1:
                        pe.wait_ge(x2_left, 1)
                        for c in range(KC // 2):
                            for t in range(NT):
                                last = turn_x2(c, t)
                            last.then_inc(h2_turned, 1)
                    if n == 1 and j == 2:
                        pe.wait_ge(wr_scaled, 1)
                        for c in range(KC // 2):
                            route_chunk(c)
                pe.wait_ge(piece_done, N_PROJ + N_UP + 4 * n + 4)
                pe.sem_inc(out_mm, 1)
            for t in range(NT):
                pe.wait_ge(x2_right, t + 1)
                for c in range(KC // 2, KC):
                    last = turn_x2(c, t)
                    if t == NT - 1:
                        last.then_inc(h2_turned, 1)
            for c in range(KC // 2, KC):
                last = route_chunk(c)
            last.then_inc(router_mm, 1)
            pe.wait_ge(logits_out, 1)
            for t in range(NT):
                last = nc.tensor.transpose(ps[:, 1, t * E:(t + 1) * E], t_po[0:E, t * P:(t + 1) * P], ident[0:E, 0:E])
            last.then_inc(logits_turned, 1)
            pe.wait_ge(mask_ready, 1)
            for t in range(NT + 1):
                o = ps[:, 7, t * E:(t + 1) * E]
                before = min(t, NT)
                for j in range(before):
                    last = m_(o, ones[:], mask[:, j, :], start=(j == 0), stop=(t == NT and j == NT - 1))
                if t < NT:
                    last = m_(o, tri[:], mask[:, t, :], start=(t == 0), stop=True)
            last.then_inc(pos_mm, 1)
            for e in range(2):
                pe.wait_ge(start_step, e + 2)
                for t in range(NT):
                    last = m_(ps[0:CAP, 5, e:e + 1], start_sel[:, e, t, :], start_tok[:, e, t:t + 1],
                              start=(t == 0), stop=(t == NT - 1))
            last.then_inc(start_mm, 1)
            pe.wait_ge(extra_fill, 1)
            for j in range(3):
                last = m_(ps[0:1, 4, j * P:(j + 1) * P], found[:, j:j + 1], ident[:], start=True, stop=True)
            last.then_inc(extra_mm, 1)

            def turn_rows(v):
                pe.wait_ge(rows_in, v * 16 + 16)
                at_least(pe, aT_lo, v - 1) if isinstance(v, int) else None
                for c in range(KC):
                    last = nc.tensor.transpose(ps[:, 6 + c // 4, (c % 4) * CAP:(c % 4 + 1) * CAP],
                                               xy[:, c * P:(c + 1) * P], ident[0:CAP, 0:CAP])
                last.then_inc(rows_turned, 1)

            def turn_act(v):
                pe.wait_ge(act_ready, v + 1)
                for c in range(KC):
                    last = nc.tensor.transpose(ps[:, 6 + c // 4, (c % 4) * CAP:(c % 4 + 1) * CAP],
                                               g_act[:, c * P:(c + 1) * P], ident[0:CAP, 0:CAP])
                last.then_inc(act_turned, 1)

            def up_bias(v):
                pe.wait_ge(sel_up_ready, v + 1)
                for n in range(4):
                    last = m_(ps[0:CAP, n, :], sel_up[:], bias[:, n * 512:(n + 1) * 512], start=True, stop=False)
                last.then_inc(up_bias_used, 1)

            def up_chunk(u, off, k):
                pe.wait_ge(elo_done, u * STEP + (off + 1))
                h = half_of(off)
                for n in range(4):
                    c = slice(n * 512, (n + 1) * 512)
                    last = three(ps[0:CAP, n, :], xeh[:, k, :], xel[:, k, :], hi[:, h, c], lo[:, h, c],
                                 False, k == DOWN - 1)
                last.then_inc(chunk_used, 1)

            def down_bias(v):
                pe.wait_ge(sel_down_ready, v + 1)
                at_least(pe, y_scaled, v)
                for n in range(2):
                    last = m_(ps[0:CAP, 4 + n, :], sel_down[:], bias[:, F2 + n * 512:F2 + (n + 1) * 512],
                              start=True, stop=False)
                last.then_inc(down_bias_used, 1)

            def down_chunk(u, off, k):
                pe.wait_ge(elo_done, u * STEP + (off + 1))
                h = half_of(off)
                for cc in range(2):
                    for n in range(2):
                        c = slice(cc * D + n * 512, cc * D + (n + 1) * 512)
                        last = three(ps[0:CAP, 4 + n, :], aTh[:, 2 * k + cc, :], aTl[:, 2 * k + cc, :],
                                     hi[:, h, c], lo[:, h, c], False, k == 3 and cc == 1)
                last.then_inc(chunk_used, 1)

            def product_done(which, u, off):
                pe.wait_ge(chunk_used, u * STEP + (off + 1))
                pe.sem_inc(which, 1)

            turn_rows(0)
            pe.wait_ge(bias_lo, 1)
            pe.wait_ge(xe_lo, 1)
            up_bias(0)
            for k in range(DOWN):
                if k == 5:
                    turn_rows(1)
                up_chunk(0, k, k)
            product_done(gu_done, 0, DOWN - 1)

            def step(u, last=False):
                pe.wait_ge(xe_lo, u + 1)
                pe.wait_ge(u_clip, u)
                up_bias(u)
                for k in range(DOWN):
                    if k == 2:
                        turn_act(u - 1)
                    up_chunk(u, k - 4, k)
                product_done(gu_done, u, DOWN - 1 - 4)
                pe.wait_ge(aT_lo, u)
                down_bias(u - 1)
                for k in range(4):
                    if k == 1 and not last:
                        turn_rows(u + 1)
                    down_chunk(u, k + 4, k)
                product_done(down_done, u, DOWN - 1)

            pe.wait_ge(extra_ready, 1)
            step(1)
            with pe.Fori(2, E - 1) as u:
                step(u)
            step(E - 1, last=True)
            turn_act(E - 1)
            pe.wait_ge(aT_lo, E)
            down_bias(E - 1)
            for k in range(4):
                down_chunk(E, k - 4, k)
            product_done(down_done, E, -1)
            n_extra = pe.value_load(extra_list[0:1, 2, 0:1], min_val=0, max_val=EXTRA)
            with pe.If(0 < n_extra):
                with pe.Fori(0, EXTRA) as i:
                    with pe.If(i < n_extra):
                        v = i + E
                        turn_rows(v)
                        pe.wait_ge(xe_lo, v + 1)
                        pe.wait_ge(u_clip, v)
                        up_bias(v)
                        for k in range(DOWN):
                            up_chunk(v, k, k)
                        product_done(gu_done, v, DOWN - 1)
                        turn_act(v)
                        pe.wait_ge(aT_lo, v + 1)
                        down_bias(v)
                        for k in range(4):
                            down_chunk(v, k + DOWN, k)
                        product_done(down_done, v, STEP - 1)


_INS = ["x", "norm_mix", "w_in", "w_pool", "pool_scale", "w_attn_up", "w_pool_up", "w_out", "norm_ffn",
        "w_router", "b_router", "w_gate_up", "b_gate_up", "w_down", "b_down", "norm_final"]


def kernel(**inputs):
    import numpy as _np
    import concourse.bacc as _bacc
    from concourse.bass_utils import run_bass_kernel_spmd as _run

    nc = _bacc.Bacc("TRN2", target_bir_lowering=False, num_devices=1)
    arrays, args = {}, []
    for name in _INS:
        a = _np.ascontiguousarray(inputs[name])
        arrays[f"in_{name}_dram"] = a
        args.append(nc.dram_tensor(f"in_{name}_dram", a.shape, mybir.dt.from_np(a.dtype), kind="ExternalInput").ap())
    _, t, d = inputs["x"].shape
    e = inputs["w_router"].shape[2]
    blocks = -(-t // CAP)
    args.append(nc.dram_tensor("h2_dram", (t, d), F32, kind="Internal").ap())
    args.append(nc.dram_tensor("table_dram", (blocks * CAP * e, 4), U32, kind="Internal").ap())
    args.append(nc.dram_tensor("y_dram", (t * TOPE + CAP, d), F32, kind="Internal").ap())
    args.append(nc.dram_tensor("out_dram", inputs["x"].shape, F32, kind="ExternalOutput").ap())
    hybrid_block(nc, *args)
    r = _run(nc, [arrays], core_ids=[0])
    return r.results[0]["out_dram"]
```

```python
from contextlib import ExitStack

import concourse.bass as bass
from concourse import mybir

ALU = mybir.AluOpType
ACT = mybir.ActivationFunctionType
AX_X = mybir.AxisListType.X
F32 = mybir.dt.float32
BF16 = mybir.dt.bfloat16
F32R = mybir.dt.float32r
I32 = mybir.dt.int32
U32 = mybir.dt.uint32

P = 128
CAP = 96
NH, DH = 8, 64
NI, DI = 8, 32
TOPK_KEYS_MAX = 256
WINDOWS = (2, 4, 8, 16)
TOPE = 4
ALPHA, LIMIT = 1.702, 7.0
EPS = 1e-5
NEG = -1e30
TAKEN = -3e38
PAD = WINDOWS[-1]
RING = 12
SPLIT = 3


def hybrid_block(nc, x, norm_mix, w_in, w_pool, pool_scale, w_attn_up, w_pool_up, w_out, norm_ffn,
                 w_router, b_router, w_gate_up, b_gate_up, w_down, b_down, norm_final,
                 h2_dram, table_dram, y_dram, late0_dram, late1_dram, extra_dram, out):
    _, T, D = x.shape
    E = w_router.shape[2]
    F2 = w_gate_up.shape[3]
    F = F2 // 2
    NT = T // P
    KC = D // P
    AW = NH * DH
    NG = len(WINDOWS)
    NKEYS = min(TOPK_KEYS_MAX, T // 4)
    NROUND = NKEYS // 8
    BLOCKS = -(-T // CAP)
    SLOTS = BLOCKS * CAP
    EXTRA = T * TOPE // CAP
    CAND = E * (BLOCKS - 1)
    KVCOL = AW
    IQCOL = KVCOL + 2 * DH
    IKCOL = IQCOL + NI * DI
    UCOL = IKCOL + DI + NI
    GCOL = UCOL + NG * P
    Q_PIECES, U_PIECE, G_PIECE = AW // P, 8, 12
    N_PROJ = G_PIECE + 2 * KC
    N_AHEAD = N_PROJ - 2 * NT
    N_UP = KC
    N_OUT = 2 * (KC // 2)
    N_PIECES = N_PROJ + N_UP + N_OUT
    STEP = 12
    assert KC == 8 and NT == 4 and F == D and NKEYS == P and DH == 64 and NG == NT and 2 * E == 64

    x_t = x[0].rearrange("(t p) d -> t p d", p=P)
    out_t = out[0].rearrange("(t p) d -> t p d", p=P)
    w_in_c = w_in[0].rearrange("(c p) n -> p c n", p=P)
    w_au_c = w_attn_up[0].rearrange("(c p) n -> p c n", p=P)
    w_pu_c = w_pool_up[0].rearrange("(c p) n -> p c n", p=P)
    w_out_c = w_out[0].rearrange("(c p) n -> p c n", p=P)
    w_gu_c = w_gate_up[0].rearrange("e (c p) n -> p e c n", p=P)
    w_dn_c = w_down[0].rearrange("e (c p) n -> p e c n", p=P)
    h2_t = h2_dram.rearrange("(t p) d -> t p d", p=P)
    y_t = y_dram[0:T * TOPE, :].rearrange("(t p k) d -> t p (k d)", p=P, k=TOPE)
    extra_t = extra_dram[0:T * TOPE, :].rearrange("(t p k) d -> t p (k d)", p=P, k=TOPE)
    extra_z = extra_dram[0:T * TOPE, :].rearrange("(n p) d -> p n d", p=E * 2)
    y_zero = y_dram[0:T * TOPE, :].rearrange("(n t p) d -> n p t d", t=NT, p=P)
    late = [late0_dram, late1_dram]
    late_t = [d[0:T, :].rearrange("(t p) d -> p t d", p=P) for d in late]
    table_init = table_dram.rearrange("(b s e) w -> s b (e w)", b=BLOCKS, e=E)
    table_blk = table_dram.rearrange("(b s e) w -> s b e w", b=BLOCKS, e=E)
    DOWN = STEP - 4

    with ExitStack() as ctx:
        def sem(name):
            return ctx.enter_context(nc.semaphore(name))

        def place(stack, name, shape, dt=F32):
            return stack.enter_context(nc.sbuf_tensor(name, shape, dt))

        ps = ctx.enter_context(nc.psum_tensor("ps", [P, 8, 512], F32))

        ident = place(ctx, "ident", [P, P])
        expert_id = place(ctx, "expert_id", [2 * E, E])
        sel_up = place(ctx, "sel_up", [2 * E, CAP], F32R)
        sel_down = place(ctx, "sel_down", [2 * E, CAP], F32R)
        gather_tab = place(ctx, "gather_tab", [CAP, 4], U32)
        y_tab = place(ctx, "y_tab", [CAP, 4], U32)
        extra_list = place(ctx, "extra_list", [1, 3, 32], I32)
        sums = place(ctx, "sums", [P, 3, NT])
        half_sums = place(ctx, "half_sums", [P, NT])
        rstd = place(ctx, "rstd", [P, 3, NT])
        half = place(ctx, "half", [P, 1])
        payload = place(ctx, "payload", [P, NT * TOPE, 4], U32)
        dest = place(ctx, "dest", [P, NT * TOPE], U32)
        start_tab = place(ctx, "start_tab", [CAP, 2], U32)

        with ExitStack() as a1:
            xTh = place(a1, "xTh", [P, KC, T], F32R)
            xTl = place(a1, "xTl", [P, KC, T], F32R)
            gates = place(a1, "gates", [P, 2 * KC, T])
            wraw = place(a1, "wraw", [P, 2, 4096])
            prob = place(a1, "prob", [P, 2, 4, T])
            with ExitStack() as a0:
                whi = place(a0, "whi", [P, 4, 1024], F32R)
                wlo = place(a0, "wlo", [P, 4, 1024], F32R)
            h2T_right = place(a1, "h2T_right", [P, KC // 2, T])
            h2N = place(a1, "h2N", [P, NT, D])
            place(a1, "rest_of_wlo", [P, 2, 1024])
            with ExitStack() as par:
                g_ffn = place(par, "g_ffn", [P, D])
                wr = place(par, "wr", [P, KC, E])
                wp = place(par, "wp", [P, NG, P])
                br = place(par, "br", [P, E])
                g_mix = place(par, "g_mix", [P, KC])
                g_ffc = place(par, "g_ffc", [P, KC])
                p_scale = place(par, "p_scale", [P, NG])
                diag = place(par, "diag", [P, P])
                tri = place(par, "tri", [P, P], BF16)
                ones = place(par, "ones", [P, P], BF16)
                e_row = place(par, "e_row", [P, E])
                with ExitStack() as a2:
                    qT = place(a2, "qT", [P, Q_PIECES, T])
                    kT = place(a2, "kT", [P, T])
                    with ExitStack() as a5:
                        vT = place(a5, "vT", [P, T])
                        iqT = place(a5, "iqT", [P, 2, T])
                        ikT = place(a5, "ikT", [P, T])
                    yT = place(a2, "yT", [P, 4, T])
                    uT = place(a2, "uT", [P, NG, PAD + T])
                    win = place(a2, "win", [P, 2, PAD + T])
                    inv_n = place(a2, "inv_n", [P, NG, PAD])
                    v_sb = place(a2, "v_sb", [P, NT, DH])
                    iw = place(a2, "iw", [P, NT, NI])
                    score = place(a2, "score", [P, NT - 1, T])
                    top8 = place(a2, "top8", [P, 8])
                    pT = place(a2, "pT", [P, 2, T])
                    yN = place(a2, "yN", [P, AW])
                    nmax = place(a2, "nmax", [P, 2, 4])
                    psumx = place(a2, "psumx", [P, 2, NH])
                    pinv = place(a2, "pinv", [P, NH])
                    zeros = place(a2, "zeros", [P, D])
                with ExitStack() as a3:
                    mTh = place(a3, "mTh", [P, KC, T], F32R)
                    mTl = place(a3, "mTl", [P, KC, T], F32R)
                    t_at = place(a3, "t_at", [P, T])
                    t_po = place(a3, "t_po", [P, T])
                    h2T_left = place(a3, "h2T_left", [P, KC // 2, T])
                with ExitStack() as a4:
                    limit = place(a4, "limit", [P, CAND])
                    code = place(a4, "code", [P, 2, CAND])
                    over = place(a4, "over", [P, CAND])
                    rank = place(a4, "rank", [P, CAND])
                    picked = place(a4, "picked", [P, CAND])
                    pick2 = place(a4, "pick2", [P, 2, CAND])
                    rank_id = place(a4, "rank_id", [P, 1])
                    found = place(a4, "found", [P, 3])
                    cnt = place(a4, "cnt", [P, E])
                    prod = place(a4, "prod", [P, NT * TOPE, E])
                    dest_f = place(a4, "dest_f", [P, NT * TOPE])
                    lg = place(a4, "lg", [P, NT, E])
                    v8 = place(a4, "v8", [P, NT, 8])
                    i8 = place(a4, "i8", [P, NT, 8], U32)
                    i4 = place(a4, "i4", [P, NT * TOPE])
                    hot = place(a4, "hot", [P, NT * TOPE, E])
                    mask = place(a4, "mask", [P, NT, E], BF16)
                    dpos = place(a4, "dpos", [P, NT, E])
                    nv0 = place(a4, "nv0", [P, NT])
                    ex = place(a4, "ex", [P, NT, TOPE])
                    exs = place(a4, "exs", [P, NT])
                    exr = place(a4, "exr", [P, NT])
                    token_id = place(a4, "token_id", [P, NT])
                    place_id = place(a4, "place_id", [P, CAP])
                    start_tok = place(a4, "start_tok", [P, 2, NT])
                    start_sel = place(a4, "start_sel", [P, 2, NT, CAP])
        hN = gates[:, 0:KC, :].rearrange("p a b -> p (a b)").rearrange("p (t d) -> p t d", t=NT)
        xN = gates[:, KC:2 * KC, :].rearrange("p a b -> p (a b)").rearrange("p (t d) -> p t d", t=NT)
        table0 = prob[0:CAP, 1, :, :].rearrange("p a b -> p (a b)")[:, 0:BLOCKS * E * 4].bitcast(U32).rearrange("s (b e w) -> s b e w", b=BLOCKS, e=E)

        with ExitStack() as f1:
            raw = place(f1, "raw", [P, RING, 2048])
            X = place(f1, "X", [P, NT, D])
            hi = place(f1, "hi", [P, SPLIT, 2048], F32R)
            lo = place(f1, "lo", [P, SPLIT, 2048], F32R)
            xy = place(f1, "xy", [CAP, D])
            xeh = place(f1, "xeh", [P, KC, CAP], F32R)
            xel = place(f1, "xel", [P, KC, CAP], F32R)
            gu = place(f1, "gu", [CAP, 3, F])
            aTh = place(f1, "aTh", [P, KC, CAP], F32R)
            aTl = place(f1, "aTl", [P, KC, CAP], F32R)
            bias = place(f1, "bias", [2 * E, F2 + D], F32R)
        bias_raw = gu[0:2 * E, :, :].rearrange("p a b -> p (a b)")
        g_lin, g_act, u_lin = gu[:, 0, :], gu[:, 1, :], gu[:, 2, :]
        ytile = [raw[:, 2 * t:2 * t + 2, :].rearrange("p a b -> p (a b)") for t in range(NT)]
        late_rows = [ytile[r].rearrange("p (t d) -> p t d", t=NT) for r in range(2)]
        o_rows = ytile[2].rearrange("p (t d) -> p t d", t=NT)
        g_fin = ytile[3][:, 0:D]

        x_in = [sem(f"x_in{t}") for t in range(NT)]
        small_in = sem("small_in")
        g_mix_in = sem("g_mix_in")
        wgroup_in = [sem("wgroup_in0"), sem("wgroup_in1")]
        const_ready = sem("const_ready")
        inv_ready = sem("inv_ready")
        tri_step = sem("tri_step")
        diag_step = sem("diag_step")
        id_step = sem("id_step")
        tab_set = sem("tab_set")
        table_inited = sem("table_inited")
        squares = sem("squares")
        mean_ready = sem("mean_ready")
        rstd_ready = sem("rstd_ready")
        h_ready = sem("h_ready")
        h_turned = sem("h_turned")
        xT_hi = sem("xT_hi")
        xT_lo = sem("xT_lo")
        hi_done = sem("hi_done")
        lo_done = sem("lo_done")
        piece_done = sem("piece_done")
        evac_dve = sem("evac_dve")
        evac_act = sem("evac_act")
        v_turned = sem("v_turned")
        v_ready = sem("v_ready")
        idx_done = sem("idx_done")
        relu_done = sem("relu_done")
        score_step = sem("score_step")
        topk_step = sem("topk_step")
        win_step = sem("win_step")
        pooled = sem("pooled")
        pool_mixed = sem("pool_mixed")
        pool_hi = sem("pool_hi")
        pool_lo = sem("pool_lo")
        logits_done = sem("logits_done")
        masked = sem("masked")
        max_found = sem("max_found")
        nmax_ready = sem("nmax_ready")
        exp_done = sem("exp_done")
        p_turned = sem("p_turned")
        pT_out = sem("pT_out")
        pv_done = sem("pv_done")
        pinv_ready = sem("pinv_ready")
        y_norm = sem("y_norm")
        y_turned = sem("y_turned")
        y_kept = sem("y_kept")
        y_hi = sem("y_hi")
        y_lo = sem("y_lo")
        gated_a = sem("gated_a")
        gated_p = sem("gated_p")
        mix_sum = sem("mix_sum")
        mT_hi = sem("mT_hi")
        mT_lo = sem("mT_lo")
        x_again = sem("x_again")
        out_mm = sem("out_mm")
        x2_left = sem("x2_left")
        x2_right = sem("x2_right")
        half_squares = sem("half_squares")
        half_mean = sem("half_mean")
        wr_scaled = sem("wr_scaled")
        logits_out = sem("logits_out")
        logits_turned = sem("logits_turned")
        h2_ready = sem("h2_ready")
        h2_stored = sem("h2_stored")
        h2_turned = sem("h2_turned")
        router_mm = sem("router_mm")
        route = sem("route")
        exp_gate = sem("exp_gate")
        mask_ready = sem("mask_ready")
        pos_mm = sem("pos_mm")
        payload_ready = sem("payload_ready")
        payload_set = sem("payload_set")
        start_step = sem("start_step")
        start_mm = sem("start_mm")
        start_ready = sem("start_ready")
        table_done = sem("table_done")
        extra_step = sem("extra_step")
        extra_mm = sem("extra_mm")
        extra_ready = sem("extra_ready")
        bias_in = sem("bias_in")
        bias_hi = sem("bias_hi")
        bias_lo = sem("bias_lo")
        raw_in = [sem(f"raw_in{s}") for s in range(RING)]
        ehi_done = sem("ehi_done")
        elo_done = sem("elo_done")
        chunk_used = sem("chunk_used")
        up_bias_used = sem("up_bias_used")
        down_bias_used = sem("down_bias_used")
        sel_up_ready = sem("sel_up_ready")
        sel_down_ready = sem("sel_down_ready")
        zeros_set = sem("zeros_set")
        zeros_out = sem("zeros_out")
        late_out = sem("late_out")
        late0_in = sem("late0_in")
        late1_in = [sem(f"late1_in{t}") for t in range(NT)]
        late_sum = sem("late_sum")
        extra_zero = sem("extra_zero")
        extra_zero_out = sem("extra_zero_out")
        extra_all = sem("extra_all")
        extra_out = sem("extra_out")
        extra_in = sem("extra_in")
        extra_added = sem("extra_added")
        pool_held = sem("pool_held")
        pair_sum = sem("pair_sum")
        pu_in = [sem("pu_in0"), sem("pu_in1")]
        h2T_act = sem("h2T_act")
        h2T_dve = sem("h2T_dve")
        extra_fill = sem("extra_fill")
        inv_step = sem("inv_step")
        mask_out = sem("mask_out")
        diag_added = sem("diag_added")
        gtab_in = sem("gtab_in")
        ytab_in = sem("ytab_in")
        rows_in = sem("rows_in")
        rows_turned = sem("rows_turned")
        xe_hi = sem("xe_hi")
        xe_lo = sem("xe_lo")
        gu_done = sem("gu_done")
        g_clip = sem("g_clip")
        u_clip = sem("u_clip")
        g_sig = sem("g_sig")
        u_one = sem("u_one")
        g_gated = sem("g_gated")
        act_ready = sem("act_ready")
        act_turned = sem("act_turned")
        aT_hi = sem("aT_hi")
        aT_lo = sem("aT_lo")
        down_done = sem("down_done")
        y_scaled = sem("y_scaled")
        y_out = sem("y_out")
        yt_in = [sem(f"yt_in{t}") for t in range(NT)]
        gfin_in = sem("gfin_in")
        comb = sem("comb")
        o_ready = sem("o_ready")
        out_stored = sem("out_stored")

        block = ctx.enter_context(nc.Block())

        def raw_piece(i):
            group = wraw[:, (i // 4) % 2, :].rearrange("p (c n) -> p c n", c=KC)
            j = i % 4
            if i < N_PROJ + N_UP:
                return group[:, :, j * P:(j + 1) * P]
            return group[:, 2 * j:2 * j + 2, :]

        def split_piece(w, i):
            n = KC if i < N_PROJ + N_UP else 2
            return w[:, i % 4, :].rearrange("p (c n) -> p c n", c=n)

        def slot_of(off):
            return off % RING

        def half_of(off):
            return off % SPLIT

        def at_least(eng, which, value):
            if not (isinstance(value, int) and value <= 0):
                eng.wait_ge(which, value)

        attn = [(t, g) for t in range(NT) for g in range(2)]
        blocks_to = [0]
        for t, _ in attn:
            blocks_to.append(blocks_to[-1] + t + 1)
        N_PT = blocks_to[-1]

        FIRST_LOGITS = N_AHEAD - 4

        def selected(t):
            m = diag[:] if t == 0 else score[:, t - 1, 0:P * (t + 1)]
            return m.unsqueeze(1).to_broadcast([P, 4, P * (t + 1)])

        def turn_bank(c):
            return 4 + c if c < KC // 2 else (c + 1) % 8

        def h2T(c):
            return h2T_left[:, c, :] if c < KC // 2 else h2T_right[:, c - KC // 2, :]

        @block.sync
        def _(sp):
            for t in range(NT):
                sp.dma_start(xN[:, t, :], x_t[t]).then_inc(x_in[t], 16)

            def group(g):
                if g >= 2:
                    sp.wait_ge(lo_done, 4 * (g - 1))
                dst = wraw[:, g % 2, :].rearrange("p (c n) -> p c n", c=KC)
                done = wgroup_in[g % 2]
                if g < 2:
                    sp.dma_start(dst, w_in_c[:, :, 512 * g:512 * g + 512]).then_inc(done, 16)
                elif g < 7:
                    c0 = UCOL + 512 * (g - 2)
                    sp.dma_start(dst, w_in_c[:, :, c0:c0 + 512]).then_inc(done, 16)
                elif g < 9:
                    c0 = 512 * (g - 7)
                    sp.dma_start(dst[:, 0:4, :], w_au_c[:, :, c0:c0 + 512]).then_inc(done, 16)
                    sp.dma_start(dst[:, 4:8, :], w_pu_c[:, :, c0:c0 + 512]).then_inc(pu_in[g - 7], 16)
                else:
                    c0 = 512 * (g - 9)
                    sp.dma_start(dst, w_out_c[:, :, c0:c0 + 512]).then_inc(done, 16)

            sp.dma_start(g_mix[:], norm_mix[0].rearrange("(c p) -> p c", p=P),
                         allow_slow_non_contiguous=True).then_inc(g_mix_in, 16)
            group(0)
            sp.dma_start(g_ffc[:], norm_ffn[0].rearrange("(c p) -> p c", p=P),
                         allow_slow_non_contiguous=True).then_inc(small_in, 16)
            sp.dma_start(p_scale[:], pool_scale[0].rearrange("(c p) -> p c", p=P),
                         allow_slow_non_contiguous=True).then_inc(small_in, 16)
            sp.dma_start(wp[:], w_pool[0].rearrange("g c d -> c g d")).then_inc(small_in, 16)
            sp.dma_start(wr[:], w_router[0].rearrange("(c p) e -> p c e", p=P)).then_inc(small_in, 16)
            sp.dma_start(br[:], b_router[0].partition_broadcast(P)).then_inc(small_in, 16)
            sp.dma_start(g_ffn[:], norm_ffn[0].partition_broadcast(P)).then_inc(small_in, 16)
            for g in range(1, 7):
                group(g)
            sp.wait_ge(zeros_set, 1)
            z = zeros[:].unsqueeze(1).to_broadcast([P, NT, D])
            for k in range(TOPE):
                sp.dma_start(y_zero[k], z).then_inc(zeros_out, 16)
            for r in range(2):
                sp.dma_start(late_t[r], z).then_inc(zeros_out, 16)
            for g in range(7, 9):
                group(g)
            sp.wait_ge(zeros_out, 16 * (TOPE + 2))
            sp.wait_ge(p_turned, N_PT)
            for t in range(NT):
                sp.dma_start(X[:, t, :], x_t[t]).then_inc(x_again, 16)
            for g in range(9, 11):
                group(g)

            def load_up(e, k, u, off):
                at_least(sp, elo_done, u * STEP + (off - RING + 1))
                sp.dma_start(raw[:, slot_of(off), :].unsqueeze(1), w_gu_c[:, bass.ds(e, 1), k, :])\
                  .then_inc(raw_in[slot_of(off)], 16)

            def load_down(e, k, u, off):
                at_least(sp, elo_done, u * STEP + (off - RING + 1))
                sp.dma_start(raw[:, slot_of(off), :].rearrange("p (a c n) -> p a c n", a=1, c=2),
                             w_dn_c[:, bass.ds(e, 1), 2 * k:2 * k + 2, :]).then_inc(raw_in[slot_of(off)], 16)

            sp.wait_ge(piece_done, N_PROJ + N_UP)
            sp.wait_ge(mix_sum, N_UP)
            for k in range(DOWN):
                load_up(0, k, 0, k)
            sp.wait_ge(lo_done, N_PIECES)
            for k in range(4):
                load_up(1, k, 1, k - 4)
            sp.wait_ge(out_mm, 2)
            for half_rows in range(2):
                r = slice(E * half_rows, E * half_rows + E)
                sp.dma_start(bias_raw[r, 0:F2], b_gate_up[0]).then_inc(bias_in, 16)
                sp.dma_start(bias_raw[r, F2:F2 + D], b_down[0]).then_inc(bias_in, 16)
            for t in range(NT):
                sp.wait_ge(h2_ready, t + 1)
                sp.dma_start(h2_t[t], h2N[:, t, :]).then_inc(h2_stored, 16)
            for k in range(4, DOWN):
                load_up(1, k, 1, k - 4)
            for k in range(4):
                load_down(0, k, 1, k + 4)
            with sp.Fori(2, E) as u:
                for k in range(DOWN):
                    load_up(u, k, u, k - 4)
                for k in range(4):
                    load_down(u - 1, k, u, k + 4)
            for k in range(4):
                load_down(E - 1, k, E, k - 4)
            sp.wait_ge(y_out, 16 * (E - 2))
            for t in range(NT):
                sp.wait_ge(elo_done, STEP * (E - 1) + 2 * t + 2)
                sp.dma_start(ytile[t], y_t[t]).then_inc(yt_in[t], 16)
            sp.wait_ge(extra_ready, 1)
            n_extra = sp.value_load(extra_list[0:1, 2, 0:1], min_val=0, max_val=EXTRA)
            with sp.If(0 < n_extra):
                sp.wait_ge(comb, 3 * NT)
                with sp.Fori(0, EXTRA) as i:
                    with sp.If(i < n_extra):
                        e = sp.value_load(extra_list[0:1, 0, bass.ds(i, 1)], min_val=0, max_val=E - 1)
                        for k in range(DOWN):
                            load_up(e, k, i + E, k)
                        for k in range(4):
                            load_down(e, k, i + E, k + DOWN)
                sp.wait_ge(extra_all, 1)
                for t in range(NT):
                    sp.dma_start(ytile[t], extra_t[t]).then_inc(extra_in, 16)
                sp.wait_ge(extra_added, NT * TOPE)
            sp.wait_ge(comb, 3)
            sp.wait_ge(late_out, 16)
            sp.dma_start(late_rows[0], late_t[0]).then_inc(late0_in, 16)
            sp.wait_ge(comb, 3 * NT)
            sp.dma_start(g_fin, norm_final.partition_broadcast(P)).then_inc(gfin_in, 16)
            sp.wait_ge(late_out, 32)
            for t in range(NT):
                sp.dma_start(late_rows[1][:, t, :], late_t[1][:, t, :]).then_inc(late1_in[t], 16)
            for t in range(NT):
                sp.wait_ge(o_ready, t + 1)
                sp.dma_start(out_t[t], o_rows[:, t, :]).then_inc(out_stored, 16)
            sp.wait_ge(out_stored, 16 * NT)

        @block.gpsimd
        def _(pool):
            g = nc.gpsimd

            def mean_rstd(r, t):
                pool.wait_ge(squares, NT * r + t + 1)
                g.tensor_scalar(sums[:, r, t:t + 1], sums[:, r, t:t + 1], 1.0 / D, EPS, ALU.mult, ALU.add)\
                 .then_inc(mean_ready, 1)
                pool.wait_ge(mean_ready, NT * r + t + 1)
                g.tensor_tensor(rstd[:, r, t:t + 1], sums[:, r, t:t + 1], half[:], ALU.pow).then_inc(rstd_ready, 1)

            g.memset(half[:], -0.5)
            g.memset(zeros[:], 0.0).then_inc(zeros_set, 1)
            g.memset(ident[:], 0.0).then_inc(id_step, 1)
            pool.wait_ge(id_step, 1)
            g.affine_select(out=ident[:], in_=ident[:], compare_op=ALU.not_equal, fill=1.0, base=0,
                            pattern=[[-1, P]], channel_multiplier=1).then_inc(id_step, 1)
            for t in range(NT):
                mean_rstd(0, t)
            g.memset(table0, 0).then_inc(tab_set, 1)
            pool.wait_ge(tab_set, 1)
            g.iota(table0[:, :, :, 1], [[0, BLOCKS], [0, E]], base=T * TOPE, channel_multiplier=1)
            g.iota(table0[:, :, :, 3], [[0, BLOCKS], [0, E]], base=T, channel_multiplier=1).then_inc(tab_set, 1)
            pool.wait_ge(tab_set, 2)
            pool.dma_start(table_init, table0.rearrange("s b e w -> s b (e w)")).then_inc(table_inited, 16)
            g.memset(diag[:], 0.0).then_inc(diag_step, 1)
            pool.wait_ge(diag_step, 1)
            g.affine_select(out=diag[:], in_=diag[:], compare_op=ALU.is_ge, fill=NEG, base=0,
                            pattern=[[-1, P]], channel_multiplier=1).then_inc(diag_step, 1)
            g.memset(ones[:], 1.0)
            g.memset(tri[:], 1.0).then_inc(tri_step, 1)
            pool.wait_ge(tri_step, 1)
            g.affine_select(out=tri[:], in_=tri[:], compare_op=ALU.is_gt, fill=0.0, base=0,
                            pattern=[[1, P]], channel_multiplier=-1)
            g.iota(e_row[:], [[1, E]], base=0, channel_multiplier=0, allow_small_or_imprecise_dtypes=True)
            g.iota(inv_n[:], [[0, NG], [1, PAD]], base=1, channel_multiplier=0,
                   allow_small_or_imprecise_dtypes=True)
            g.memset(expert_id[:], 0.0).then_inc(tri_step, 1)
            for r in range(2):
                pool.wait_ge(tri_step, 2 + r)
                g.affine_select(out=expert_id[:], in_=expert_id[:], compare_op=ALU.not_equal, fill=1.0,
                                base=-E * r, pattern=[[-1, E]], channel_multiplier=1).then_inc(tri_step, 1)
            g.memset(uT[:, :, 0:PAD], 0.0)
            g.memset(win[:, :, 0:PAD], 0.0).then_inc(const_ready, 1)
            pool.wait_ge(const_ready, 1)
            pool.wait_ge(inv_ready, NG)
            steps = 0
            for j, w in enumerate(WINDOWS):
                pool.wait_ge(evac_act, j + 1)
                src = uT[:, j, :]
                for lv in range(j + 1):
                    if steps:
                        pool.wait_ge(win_step, steps)
                    dst = win[:, lv % 2, :]
                    sh = 1 << lv
                    g.tensor_tensor(dst[:, PAD:], src[:, PAD:], src[:, PAD - sh:PAD + T - sh], ALU.add)\
                     .then_inc(win_step, 1)
                    steps += 1
                    src = dst
                pool.wait_ge(win_step, steps)
                g.tensor_scalar(src[:, 2 * PAD:], src[:, 2 * PAD:], 1.0 / w, None, ALU.mult)
                g.tensor_tensor(src[:, PAD:2 * PAD], src[:, PAD:2 * PAD], inv_n[:, j, :], ALU.mult).then_inc(win_step, 1)
                steps += 1
                pool.wait_ge(win_step, steps)
                g.tensor_tensor(uT[:, j, PAD:], src[:, PAD:], uT[:, j, PAD:], ALU.subtract).then_inc(pooled, 1)
                pool.wait_ge(pooled, j + 1)
            g.memset(payload[:], 0).then_inc(tab_set, 1)
            pool.wait_ge(tab_set, 3)
            pv = payload[:].rearrange("p (t k) w -> p t k w", t=NT)
            g.iota(pv[:, :, :, 0], [[P, NT], [0, TOPE]], base=0, channel_multiplier=1)
            g.iota(pv[:, :, :, 3], [[P, NT], [0, TOPE]], base=0, channel_multiplier=1)
            g.iota(pv[:, :, :, 1], [[P * TOPE, NT], [1, TOPE]], base=0, channel_multiplier=TOPE)
            pool.wait_ge(half_squares, NT)
            g.tensor_scalar(half_sums[:], half_sums[:], EPS, None, ALU.add).then_inc(half_mean, 1)
            pool.wait_ge(half_mean, 1)
            for t in range(NT):
                pool.wait_ge(squares, NT + t + 1)
                g.tensor_tensor(sums[:, 1, t:t + 1], sums[:, 1, t:t + 1], half_sums[:, t:t + 1], ALU.add)\
                 .then_inc(mean_ready, 1)
                pool.wait_ge(mean_ready, NT + t + 1)
                g.tensor_tensor(rstd[:, 1, t:t + 1], sums[:, 1, t:t + 1], half[:], ALU.pow).then_inc(rstd_ready, 1)
            pool.wait_ge(out_mm, 2)
            g.iota(token_id[:], [[P, NT]], base=0, channel_multiplier=1, allow_small_or_imprecise_dtypes=True)
            g.iota(place_id[:], [[1, CAP]], base=0, channel_multiplier=0, allow_small_or_imprecise_dtypes=True)
            g.iota(limit[:], [[0, E], [CAP, BLOCKS - 1]], base=CAP, channel_multiplier=0,
                   allow_small_or_imprecise_dtypes=True)
            g.iota(code[:, 0, :], [[1, E], [0, BLOCKS - 1]], base=0, channel_multiplier=0,
                   allow_small_or_imprecise_dtypes=True)
            g.iota(code[:, 1, :], [[0, E], [1, BLOCKS - 1]], base=1, channel_multiplier=0,
                   allow_small_or_imprecise_dtypes=True)
            g.memset(picked[:], 1.0)
            g.iota(rank_id[:], [[0, 1]], base=1, channel_multiplier=1,
                   allow_small_or_imprecise_dtypes=True).then_inc(payload_set, 1)
            def table_rows(dst, e, blk):
                src = table_blk[:, bass.ds(blk, 1), bass.ds(e, 1), :]
                return pool.dma_start(dst[:].rearrange("s (b e w) -> s b e w", b=1, e=1), src)

            def hold():
                pool.sem_inc(pool_held, 1)

            def first_gather(e):
                pool.indirect_dma_start(xy[:], None, h2_dram,
                                        bass.IndirectOffsetOnAxis(start_tab[:, e:e + 1], 0)).then_inc(rows_in, 16)

            def gather(v, e, blk, load=True):
                if load:
                    table_rows(gather_tab, e, blk).then_inc(gtab_in, 16)
                pool.wait_ge(gtab_in, v * 16 - 16)
                hold()
                pool.indirect_dma_start(xy[:], None, h2_dram,
                                        bass.IndirectOffsetOnAxis(gather_tab[:, 0:1], 0)).then_inc(rows_in, 16)

            def choose_up(v, e):
                at_least(pool, up_bias_used, v)
                hold()
                g.tensor_copy(sel_up[:], expert_id[:, bass.ds(e, 1)].to_broadcast([2 * E, CAP]))\
                 .then_inc(sel_up_ready, 1)

            def choose_down(v, e):
                at_least(pool, down_bias_used, v)
                hold()
                g.tensor_copy(sel_down[:], expert_id[:, bass.ds(e, 1)].to_broadcast([2 * E, CAP]))\
                 .then_inc(sel_down_ready, 1)

            def scatter(v):
                pool.wait_ge(y_scaled, v + 1)
                hold()
                pool.indirect_dma_start(y_dram, bass.IndirectOffsetOnAxis(y_tab[:, 1:2], 0), xy[:], None)\
                    .then_inc(y_out, 16)
                pool.wait_ge(y_out, v * 16 + 16)

            def scatter_late(r):
                pool.wait_ge(y_scaled, E - 1 + r)
                pool.indirect_dma_start(late[r], bass.IndirectOffsetOnAxis(y_tab[:, 3:4], 0), xy[:], None)\
                    .then_inc(late_out, 16)

            def scatter_extra(i):
                pool.wait_ge(y_scaled, i + (E + 1))
                hold()
                pool.indirect_dma_start(extra_dram, bass.IndirectOffsetOnAxis(y_tab[:, 1:2], 0), xy[:], None)\
                    .then_inc(extra_out, 16)
                pool.wait_ge(extra_out, i * 16 + 16)

            def activation(v):
                pool.wait_ge(g_sig, v + 1)
                g.tensor_tensor(g_lin, g_lin, g_act, ALU.mult).then_inc(g_gated, 1)
                pool.wait_ge(g_gated, v + 1)
                pool.wait_ge(u_one, v + 1)
                g.tensor_tensor(g_act, g_lin, u_lin, ALU.mult).then_inc(act_ready, 1)

            pool.wait_ge(h2_stored, 16 * NT)
            pool.wait_ge(route, 3 * NT + 7)
            pool.wait_ge(start_ready, 1)
            first_gather(0)
            choose_up(0, 0)
            pool.wait_ge(table_inited, 16)
            pool.wait_ge(payload_ready, 1)
            for j in range(NT * TOPE):
                pool.indirect_dma_start(table_dram, bass.IndirectOffsetOnAxis(dest[:, j:j + 1], 0),
                                        payload[:, j, :], None).then_inc(table_done, 16)
            pool.wait_ge(rows_turned, 1)
            first_gather(1)
            choose_up(1, 1)
            choose_down(0, 0)
            activation(0)
            pool.wait_ge(zeros_out, 16 * (TOPE + 2))
            pool.wait_ge(table_done, 16 * NT * TOPE)
            table_rows(y_tab, 0, 0).then_inc(ytab_in, 16)
            pool.wait_ge(rows_turned, 2)
            gather(2, 2, 0)
            choose_up(2, 2)
            choose_down(1, 1)
            activation(1)

            def step(u, last=False):
                pool.wait_ge(rows_turned, u + 1)
                if not last:
                    table_rows(gather_tab, u + 1, 0).then_inc(gtab_in, 16)
                scatter(u - 2)
                table_rows(y_tab, u - 1, 0).then_inc(ytab_in, 16)
                if not last:
                    gather(u + 1, u + 1, 0, load=False)
                    choose_up(u + 1, u + 1)
                choose_down(u, u)
                activation(u)

            with pool.Fori(2, E - 1) as u:
                step(u)
            step(E - 1, last=True)
            def pair(t):
                pool.wait_ge(yt_in[t], 16)
                g.tensor_tensor(ytile[t][:, 3 * D:], ytile[t][:, 2 * D:3 * D], ytile[t][:, 3 * D:], ALU.add)\
                 .then_inc(pair_sum, 1)

            scatter_late(0)
            pair(0)
            pair(1)
            pool.wait_ge(late_out, 16)
            table_rows(y_tab, E - 1, 0).then_inc(ytab_in, 16)
            pair(2)
            pair(3)
            scatter_late(1)
            pool.wait_ge(late_out, 32)
            pool.wait_ge(extra_ready, 1)
            n_extra = pool.value_load(extra_list[0:1, 2, 0:1], min_val=0, max_val=EXTRA)
            with pool.If(0 < n_extra):
                g.memset(xy[0:2 * E, :], 0.0).then_inc(extra_zero, 1)
                pool.wait_ge(extra_zero, 1)
                with pool.Fori(0, T * TOPE // (2 * E)) as n:
                    pool.dma_start(extra_z[:, bass.ds(n, 1), :], xy[0:2 * E, :].unsqueeze(1)).then_inc(extra_zero_out, 16)
                pool.wait_ge(extra_zero_out, 16 * (T * TOPE // (2 * E)))
                with pool.Fori(0, EXTRA) as i:
                    with pool.If(i < n_extra):
                        e = pool.value_load(extra_list[0:1, 0, bass.ds(i, 1)], min_val=0, max_val=E - 1)
                        b = pool.value_load(extra_list[0:1, 1, bass.ds(i, 1)], min_val=0, max_val=BLOCKS - 1)
                        gather(i + E, e, b)
                        choose_up(i + E, e)
                        choose_down(i + E, e)
                        table_rows(y_tab, e, b).then_inc(ytab_in, 16)
                        activation(i + E)
                        scatter_extra(i)
                pool.sem_inc(extra_all, 1)
            for t in range(NT):
                mean_rstd(2, t)

        @block.scalar
        def _(act):
            s = nc.scalar

            def hi_part(i):
                g = i // 4
                act.wait_ge(wgroup_in[g % 2], 16 * (g // 2 + 1))
                if g in (7, 8):
                    act.wait_ge(pu_in[g - 7], 16)
                if i >= 4:
                    act.wait_ge(piece_done, i - 3)
                s.activation(split_piece(whi, i), raw_piece(i), ACT.Copy).then_inc(hi_done, 1)

            def square(r, t, src, dst):
                s.activation(dst, src, ACT.Square, accum_out=sums[:, r, t:t + 1]).then_inc(squares, 1)

            for t in range(NT):
                act.wait_ge(x_in[t], 16)
                square(0, t, xN[:, t, :], hN[:, t, :])
            act.wait_ge(g_mix_in, 16)
            for c in range(KC):
                act.wait_ge(h_turned, c + 1)
                s.activation(xTh[:, c, :], ps[:, 4 + c % 4, :], ACT.Copy, scale=g_mix[:, c:c + 1]).then_inc(xT_hi, 1)
                if c == 3:
                    hi_part(0)
            hi_part(1)
            hi_part(2)

            def relus(t, h):
                n = 2 * (t - 1) + h
                act.wait_ge(idx_done, n + 1)
                if n:
                    act.wait_ge(score_step, 4 * n)
                s.activation(prob[:, 0, :, 0:P * (t + 1)], ps[:, 2:6, 0:P * (t + 1)], ACT.Relu).then_inc(relu_done, 1)

            def exps(a):
                t, g = attn[a]
                act.wait_ge(nmax_ready, a + 1)
                for j in range(4):
                    last = s.activation(prob[:, a % 2, j, 0:P * (t + 1)], prob[:, a % 2, j, 0:P * (t + 1)], ACT.Exp,
                                        bias=nmax[:, a % 2, j:j + 1], accum_out=psumx[:, t % 2, 4 * g + j:4 * g + j + 1])
                last.then_inc(exp_done, 1)

            for i in range(N_AHEAD):
                hi_part(i + 3)
                act.wait_ge(piece_done, i + 1)
                if U_PIECE <= i < G_PIECE:
                    s.activation(uT[:, i - U_PIECE, PAD:], ps[:, i % 2, :], ACT.Copy).then_inc(evac_act, 1)
                elif i >= G_PIECE:
                    s.activation(gates[:, i - G_PIECE, :], ps[:, i % 2, :], ACT.Sigmoid).then_inc(evac_act, 1)
                if 9 <= i < 9 + 2 * (NT - 1):
                    relus(1 + (i - 9) // 2, (i - 9) % 2)
                if i == FIRST_LOGITS + 2:
                    exps(0)
            def keep_y(t):
                act.wait_ge(y_turned, t + 1)
                s.activation(yT[:, :, t * P:(t + 1) * P], ps[:, 0, :].rearrange("p (c n) -> p c n", c=4), ACT.Copy)\
                 .then_inc(y_kept, 1)

            for a, (t, g) in enumerate(attn):
                if g == 0 and t >= 1:
                    keep_y(t - 1)
                for n in range(blocks_to[a], blocks_to[a + 1]):
                    act.wait_ge(p_turned, n + 1)
                    if n >= 2:
                        act.wait_ge(pv_done, n - 1)
                    s.activation(pT[:, n % 2, :], ps[:, 6 + n % 2, :], ACT.Copy).then_inc(pT_out, 1)
                if a + 1 < len(attn):
                    exps(a + 1)
                i = N_AHEAD + a
                hi_part(i + 3)
                act.wait_ge(piece_done, i + 1)
                s.activation(gates[:, i - G_PIECE, :], ps[:, 0, :], ACT.Sigmoid).then_inc(evac_act, 1)
            act.wait_ge(y_kept, NT - 1)
            s.activation(xTh[:, 0:4, 0:T - P], yT[:, :, 0:T - P], ACT.Copy).then_inc(y_hi, 1)
            act.wait_ge(small_in, 96)
            for j in range(NG):
                act.wait_ge(pool_mixed, j + 1)
                s.activation(xTh[:, 4 + j, :], ps[:, 2 + j, :], ACT.Copy, scale=p_scale[:, j:j + 1]).then_inc(pool_hi, 1)
            act.wait_ge(y_turned, NT)
            s.activation(xTh[:, 0:4, T - P:], ps[:, 0, :].rearrange("p (c n) -> p c n", c=4), ACT.Copy).then_inc(y_hi, 1)
            for m in range(N_UP):
                hi_part(N_PROJ + m + 3)
                act.wait_ge(mix_sum, m + 1)
                s.activation(mTh[:, m, :], t_at[:], ACT.Copy).then_inc(mT_hi, 1)
            for i in range(N_PROJ + N_UP + 3, N_PIECES):
                hi_part(i)
            act.wait_ge(x2_left, 1)
            for t in range(NT):
                if t:
                    act.wait_ge(half_squares, t)
                s.activation(t_at[:], X[:, t, 0:T], ACT.Square, scale=D ** -0.5, accum_out=half_sums[:, t:t + 1])\
                 .then_inc(half_squares, 1)
            for c in range(0, KC // 2, 2):
                act.wait_ge(h2_turned, c + 1)
                s.activation(h2T(c), ps[:, turn_bank(c), :], ACT.Copy).then_inc(h2T_act, 1)
            act.wait_ge(half_squares, NT)
            for t in range(NT):
                act.wait_ge(x2_right, t + 1)
                if t:
                    act.wait_ge(squares, NT + t)
                s.activation(t_at[:], X[:, t, T:D], ACT.Square, scale=D ** -0.5, accum_out=sums[:, 1, t:t + 1])\
                 .then_inc(squares, 1)
            for c in range(KC // 2, KC, 2):
                act.wait_ge(h2_turned, c + 1)
                s.activation(h2T(c), ps[:, turn_bank(c), :], ACT.Copy).then_inc(h2T_act, 1)
            act.wait_ge(router_mm, 1)
            s.activation(t_po[0:E, :], ps[0:E, 4, :], ACT.Copy).then_inc(logits_out, 1)
            act.wait_ge(bias_in, 64)
            act.wait_ge(logits_turned, 1)
            s.activation(bias[:], bias_raw, ACT.Copy).then_inc(bias_hi, 1)
            act.wait_ge(route, 3 * NT + 2)
            for t in range(NT):
                s.activation(ex[:, t, :], v8[:, t, 0:TOPE], ACT.Exp, bias=nv0[:, t:t + 1],
                             accum_out=exs[:, t:t + 1]).then_inc(exp_gate, 1)


            def ehi(u, off):
                act.wait_ge(raw_in[slot_of(off)], u * 16 + 16 * (off // STEP + 1))
                at_least(act, chunk_used, u * STEP + (off - SPLIT + 1))
                s.activation(hi[:, half_of(off), :], raw[:, slot_of(off), :], ACT.Copy).then_inc(ehi_done, 1)

            def xe_high(v):
                at_least(act, gu_done, v)
                act.wait_ge(rows_turned, v + 1)
                s.activation(xeh[:].rearrange("p (b c) n -> p b (c n)", b=2), ps[:, 6:8, 0:4 * CAP], ACT.Copy)\
                 .then_inc(xe_hi, 1)

            def sigmoid(v):
                act.wait_ge(g_clip, v + 1)
                s.activation(g_act, g_lin, ACT.Sigmoid, scale=ALPHA).then_inc(g_sig, 1)

            def plus_one(v):
                act.wait_ge(u_clip, v + 1)
                s.activation(u_lin, u_lin, ACT.Copy, bias=1.0).then_inc(u_one, 1)

            def aT_high(v):
                act.wait_ge(act_turned, v + 1)
                s.activation(aTh[:].rearrange("p (b c) n -> p b (c n)", b=2), ps[:, 6:8, 0:4 * CAP], ACT.Copy)\
                 .then_inc(aT_hi, 1)

            def scale_y(v):
                act.wait_ge(down_done, v + 1)
                act.wait_ge(ytab_in, v * 16 + 16)
                s.activation(xy[:], ps[0:CAP, 4:6, :].rearrange("p b n -> p (b n)"), ACT.Copy,
                             scale=y_tab[:, 2:3].bitcast(F32)).then_inc(y_scaled, 1)

            def end_of_step(u, off, more=True):
                for k in (8, 9, 10):
                    ehi(u, off + k)
                sigmoid(u)
                ehi(u, off + 11)
                plus_one(u)
                if more:
                    xe_high(u + 1)

            ehi(0, 0)
            xe_high(0)
            act.wait_ge(h2_stored, 16 * NT)
            for k in range(1, DOWN):
                ehi(0, k)
            ehi(1, -4)
            ehi(1, -3)
            xe_high(1)
            sigmoid(0)
            plus_one(0)

            def step(u, first=False, last=False):
                if not first:
                    ehi(u, -4)
                    ehi(u, -3)
                    act.wait_ge(rows_turned, u + 1)
                    scale_y(u - 2)
                ehi(u, -2)
                ehi(u, -1)
                aT_high(u - 1)
                for k in range(4, DOWN):
                    ehi(u, k - 4)
                end_of_step(u, -4, more=not last)

            step(1, first=True)
            with act.Fori(2, E - 1) as u:
                step(u)
            step(E - 1, last=True)
            for k in range(SPLIT):
                ehi(E, k - 4)
                if k == 1:
                    scale_y(E - 2)
            aT_high(E - 1)
            ehi(E, SPLIT - 4)
            scale_y(E - 1)
            act.wait_ge(extra_ready, 1)
            n_extra = act.value_load(extra_list[0:1, 2, 0:1], min_val=0, max_val=EXTRA)
            with act.If(0 < n_extra):
                with act.Fori(0, EXTRA) as i:
                    with act.If(i < n_extra):
                        v = i + E
                        xe_high(v)
                        for k in range(DOWN):
                            ehi(v, k)
                        sigmoid(v)
                        plus_one(v)
                        for k in range(DOWN, STEP - 1):
                            ehi(v, k)
                        aT_high(v)
                        ehi(v, STEP - 1)
                        scale_y(v)
            for t in range(NT):
                act.wait_ge(late_sum, t + 2)
                if t >= 3:
                    act.wait_ge(squares, 2 * NT + t - 2)
                square(2, t, X[:, t, :], ytile[3][:, (t % 3 + 1) * D:(t % 3 + 2) * D])

        @block.vector
        def _(dve):
            v_ = nc.vector

            def lo_part(i):
                dve.wait_ge(hi_done, i + 1)
                v_.tensor_tensor(split_piece(wlo, i), raw_piece(i), split_piece(whi, i).bitcast(F32), ALU.subtract)\
                  .then_inc(lo_done, 1)

            for t in range(NT):
                dve.wait_ge(rstd_ready, t + 1)
                v_.tensor_scalar(hN[:, t, :], xN[:, t, :], rstd[:, 0, t:t + 1], None, ALU.mult).then_inc(h_ready, 1)
            dve.wait_ge(g_mix_in, 16)
            for c in range(KC):
                dve.wait_ge(xT_hi, c + 1)
                v_.scalar_tensor_tensor(xTl[:, c, :], ps[:, 4 + c % 4, :], g_mix[:, c:c + 1], xTh[:, c, :].bitcast(F32),
                                        ALU.mult, ALU.subtract).then_inc(xT_lo, 1)
                if c == 3:
                    lo_part(0)
            lo_part(1)
            lo_part(2)
            dve.wait_ge(small_in, 96)
            v_.tensor_tensor(wr[:], wr[:], g_ffc[:].unsqueeze(2).to_broadcast([P, KC, E]), ALU.mult)\
              .then_inc(wr_scaled, 1)
            dve.wait_ge(const_ready, 1)
            for j, w in enumerate(WINDOWS):
                v_.tensor_scalar(inv_n[:, j, :], inv_n[:, j, :], float(w), None, ALU.min).then_inc(inv_step, 1)
                dve.wait_ge(inv_step, j + 1)
                v_.reciprocal(inv_n[:, j, :], inv_n[:, j, :]).then_inc(inv_ready, 1)

            def evacuate(i):
                dve.wait_ge(piece_done, i + 1)
                src = ps[:, i % 2, :]
                if i < Q_PIECES:
                    last = v_.tensor_copy(qT[:, i, :], src)
                elif i == 4:
                    v_.tensor_copy(kT[0:DH, :], src[0:DH, :])
                    v_.tensor_copy(kT[DH:2 * DH, :], src[0:DH, :])
                    last = v_.tensor_copy(vT[DH:2 * DH, :], src[DH:2 * DH, :])
                elif i < 7:
                    last = v_.tensor_copy(iqT[:, i - 5, :], src)
                else:
                    for r in range(4):
                        v_.tensor_copy(ikT[r * DI:(r + 1) * DI, :], src[0:DI, :])
                    last = v_.tensor_copy(vT[DI:DI + NI, :], src[DI:DI + NI, :])
                last.then_inc(evac_dve, 1)

            def add_heads(t, h):
                n = 2 * (t - 1) + h
                nk = P * (t + 1)
                dve.wait_ge(relu_done, n + 1)
                if n:
                    dve.wait_ge(score_step, 4 * n)
                sc = score[:, t - 1, 0:nk]
                for j in range(4):
                    w = iw[:, t, 4 * h + j:4 * h + j + 1]
                    if h == 0 and j == 0:
                        v_.tensor_scalar(sc, prob[:, 0, j, 0:nk], w, None, ALU.mult).then_inc(score_step, 1)
                    else:
                        dve.wait_ge(score_step, 4 * n + j)
                        v_.scalar_tensor_tensor(sc, prob[:, 0, j, 0:nk], w, sc, ALU.mult, ALU.add)\
                          .then_inc(score_step, 1)
                if h == 1:
                    dve.wait_ge(score_step, 4 * n + 4)
                    v_.tensor_tensor(sc[:, t * P:], sc[:, t * P:], diag[:], ALU.add).then_inc(diag_added, 1)
                    dve.wait_ge(diag_added, t)

            rounds_done = [0]

            def topk(t, r0, r1):
                sc = score[:, t - 1, 0:P * (t + 1)]
                for r in range(r0, r1):
                    n = 2 * (NROUND * (t - 1) + r)
                    if n:
                        dve.wait_ge(topk_step, n)
                    v_.max(top8[:], sc).then_inc(topk_step, 1)
                    dve.wait_ge(topk_step, n + 1)
                    v_.match_replace(sc, top8[:], sc, TAKEN).then_inc(topk_step, 1)
                if r1 == NROUND:
                    dve.wait_ge(topk_step, 2 * NROUND * t)
                    v_.tensor_scalar(sc, sc, TAKEN / 2, NEG, ALU.is_gt, ALU.mult).then_inc(mask_out, 1)

            def mask_logits(a):
                t, g = attn[a]
                nk = P * (t + 1)
                dve.wait_ge(logits_done, a + 1)
                if a >= 2:
                    dve.wait_ge(p_turned, blocks_to[a - 1])
                if g == 0 and t >= 1:
                    dve.wait_ge(mask_out, t)
                if a == 1:
                    dve.wait_ge(table_inited, 16)
                pr = prob[:, a % 2, :, 0:nk]
                v_.scalar_tensor_tensor(pr, ps[:, 2:6, 0:nk], DH ** -0.5, selected(t), ALU.mult, ALU.add)\
                  .then_inc(masked, 1)
                dve.wait_ge(masked, a + 1)
                v_.tensor_reduce(nmax[:, a % 2, :], pr, AX_X, ALU.max).then_inc(max_found, 1)
                dve.wait_ge(max_found, a + 1)
                v_.tensor_scalar(nmax[:, a % 2, :], nmax[:, a % 2, :], -1.0, None, ALU.mult).then_inc(nmax_ready, 1)

            dve.wait_ge(diag_step, 2)
            for i in range(N_AHEAD):
                lo_part(i + 3)
                if i < U_PIECE:
                    evacuate(i)
                if i == U_PIECE:
                    dve.wait_ge(v_turned, 1)
                    v_.tensor_copy(v_sb[:], ps[:, 6, 0:NT * DH].rearrange("p (t d) -> p t d", t=NT))
                    v_.tensor_scalar(iw[:], ps[:, 6, 256:256 + NT * NI].rearrange("p (t d) -> p t d", t=NT),
                                     (NI ** -0.5) * (DI ** -0.5), None, ALU.mult).then_inc(v_ready, 1)
                    dve.wait_ge(v_ready, 1)
                if 10 <= i < 10 + 2 * (NT - 1):
                    add_heads(1 + (i - 10) // 2, (i - 10) % 2)
                if i == FIRST_LOGITS + 1:
                    mask_logits(0)
                if i in (13, 15):
                    topk(1, 8 * (i == 15), 8 + 8 * (i == 15))
                if 16 <= i < 20:
                    topk(2, 3 * (i - 16), 3 * (i - 15))
            for a, (t, g) in enumerate(attn):
                if a + 1 < len(attn):
                    mask_logits(a + 1)
                if a < 2:
                    topk(2, 12 + 2 * a, 14 + 2 * a)
                if 1 <= a < 5:
                    topk(3, (0, 2, 6, 11)[a - 1], (2, 6, 11, 16)[a - 1])
                lo_part(N_AHEAD + a + 3)
                if g == 1:
                    dve.wait_ge(exp_done, a + 1)
                    v_.reciprocal(pinv[:], psumx[:, t % 2, :]).then_inc(pinv_ready, 1)
                    dve.wait_ge(pinv_ready, t + 1)
                    dve.wait_ge(pv_done, blocks_to[a + 1])
                    if t:
                        dve.wait_ge(y_turned, t)
                    v_.tensor_tensor(yN[:].rearrange("p (h d) -> p h d", h=NH),
                                     ps[:, 1, :].rearrange("p (h d) -> p h d", h=NH),
                                     pinv[:].unsqueeze(2).to_broadcast([P, NH, DH]), ALU.mult).then_inc(y_norm, 1)
            dve.wait_ge(y_hi, 1)
            v_.tensor_tensor(xTl[:, 0:4, 0:T - P], yT[:, :, 0:T - P], xTh[:, 0:4, 0:T - P].bitcast(F32), ALU.subtract)\
              .then_inc(y_lo, 1)
            for j in range(NG):
                dve.wait_ge(pool_hi, j + 1)
                v_.scalar_tensor_tensor(xTl[:, 4 + j, :], ps[:, 2 + j, :], p_scale[:, j:j + 1],
                                        xTh[:, 4 + j, :].bitcast(F32), ALU.mult, ALU.subtract).then_inc(pool_lo, 1)
            dve.wait_ge(y_hi, 2)
            v_.tensor_tensor(xTl[:, 0:4, T - P:], ps[:, 0, :].rearrange("p (c n) -> p c n", c=4),
                             xTh[:, 0:4, T - P:].bitcast(F32), ALU.subtract).then_inc(y_lo, 1)
            for m in range(N_UP):
                lo_part(N_PROJ + m + 3)
                dve.wait_ge(piece_done, N_PROJ + m + 1)
                if m:
                    dve.wait_ge(mT_lo, m)
                b = 2 * (m % 2)
                v_.tensor_tensor(t_at[:], ps[:, b, :], gates[:, m, :], ALU.mult).then_inc(gated_a, 1)
                v_.tensor_tensor(t_po[:], ps[:, b + 1, :], gates[:, KC + m, :], ALU.mult).then_inc(gated_p, 1)
                dve.wait_ge(gated_a, m + 1)
                dve.wait_ge(gated_p, m + 1)
                v_.tensor_tensor(t_at[:], t_at[:], t_po[:], ALU.add).then_inc(mix_sum, 1)
                dve.wait_ge(mix_sum, m + 1)
                dve.wait_ge(mT_hi, m + 1)
                v_.tensor_tensor(mTl[:, m, :], t_at[:], mTh[:, m, :].bitcast(F32), ALU.subtract).then_inc(mT_lo, 1)
            for i in range(N_PROJ + N_UP + 3, N_PIECES):
                lo_part(i)
            dve.wait_ge(x_again, 16 * NT)
            dve.wait_ge(out_mm, 1)
            v_.tensor_tensor(X[:, :, 0:T], X[:, :, 0:T], ps[:, 4:8, :], ALU.add).then_inc(x2_left, 1)

            def turned_out(c):
                dve.wait_ge(h2_turned, c + 1)
                v_.tensor_copy(h2T(c), ps[:, turn_bank(c), :]).then_inc(h2T_dve, 1)

            turned_out(1)
            turned_out(3)
            dve.wait_ge(out_mm, 2)
            for t in range(NT):
                v_.tensor_tensor(X[:, t, T:D], X[:, t, T:D], ps[:, t, :], ALU.add).then_inc(x2_right, 1)
            turned_out(5)
            turned_out(7)
            dve.wait_ge(x2_left, 1)
            dve.wait_ge(x2_right, NT)
            for t in range(NT):
                dve.wait_ge(rstd_ready, NT + t + 1)
                v_.scalar_tensor_tensor(h2N[:, t, :], X[:, t, :], rstd[:, 1, t:t + 1], g_ffn[:], ALU.mult, ALU.mult)\
                  .then_inc(h2_ready, 1)
            for t in range(NT):
                dve.wait_ge(logits_turned, 1)
                v_.scalar_tensor_tensor(lg[:, t, :], ps[:, 1, t * E:(t + 1) * E], rstd[:, 1, t:t + 1], br[:],
                                        ALU.mult, ALU.add).then_inc(route, 1)
            for t in range(NT):
                dve.wait_ge(route, NT + 2 * t if t else NT)
                v_.max(v8[:, t, :], lg[:, t, :]).then_inc(route, 1)
                dve.wait_ge(route, NT + 2 * t + 1)
                v_.max_index(i8[:, t, :], v8[:, t, :], lg[:, t, :]).then_inc(route, 1)
            dve.wait_ge(route, 3 * NT)
            v_.tensor_scalar(nv0[:], v8[:, :, 0], -1.0, None, ALU.mult).then_inc(route, 1)
            v_.tensor_copy(i4[:].rearrange("p (t k) -> p t k", t=NT), i8[:, :, 0:TOPE]).then_inc(route, 1)
            dve.wait_ge(route, 3 * NT + 2)
            v_.tensor_tensor(hot[:], e_row[:].unsqueeze(1).to_broadcast([P, NT * TOPE, E]),
                             i4[:].unsqueeze(2).to_broadcast([P, NT * TOPE, E]), ALU.is_equal).then_inc(route, 1)
            dve.wait_ge(route, 3 * NT + 3)
            v_.tensor_reduce(mask[:], hot[:].rearrange("p (t k) e -> p t e k", t=NT), AX_X, ALU.max)\
              .then_inc(mask_ready, 1)
            dve.wait_ge(exp_gate, NT)
            v_.reciprocal(exr[:], exs[:]).then_inc(route, 1)
            dve.wait_ge(route, 3 * NT + 4)
            dve.wait_ge(payload_set, 1)
            v_.tensor_tensor(payload[:, :, 2].bitcast(F32).rearrange("p (t k) -> p t k", t=NT), ex[:],
                             exr[:].unsqueeze(2).to_broadcast([P, NT, TOPE]), ALU.mult).then_inc(route, 1)
            v_.tensor_tensor(start_tok[:], token_id[:].unsqueeze(1).to_broadcast([P, 2, NT]),
                             mask[:, :, 0:2].rearrange("p t e -> p e t"), ALU.mult).then_inc(start_step, 1)
            dve.wait_ge(pos_mm, 1)
            for e in range(2):
                v_.tensor_tensor(start_sel[:, e],
                                 ps[:, 7, 0:NT * E].rearrange("p (t e) -> p t e", t=NT)[:, :, e:e + 1]
                                 .to_broadcast([P, NT, CAP]),
                                 place_id[:].unsqueeze(1).to_broadcast([P, NT, CAP]), ALU.is_equal)\
                  .then_inc(start_step, 1)
            v_.scalar_tensor_tensor(dpos[:], ps[:, 7, 0:NT * E].rearrange("p (t e) -> p t e", t=NT), float(E),
                                    e_row[:].unsqueeze(1).to_broadcast([P, NT, E]), ALU.mult, ALU.add)
            v_.tensor_copy(cnt[:], ps[:, 7, NT * E:NT * E + E]).then_inc(route, 1)
            dve.wait_ge(route, 3 * NT + 6)
            v_.tensor_tensor(prod[:].rearrange("p (t k) e -> p t k e", t=NT),
                             hot[:].rearrange("p (t k) e -> p t k e", t=NT),
                             dpos[:].unsqueeze(2).to_broadcast([P, NT, TOPE, E]), ALU.mult).then_inc(route, 1)
            dve.wait_ge(start_mm, 1)
            v_.tensor_copy(start_tab[:], ps[0:CAP, 5, 0:2]).then_inc(start_ready, 1)
            dve.wait_ge(route, 3 * NT + 7)
            v_.tensor_reduce(dest_f[:], prod[:], AX_X, ALU.add).then_inc(route, 1)
            dve.wait_ge(route, 3 * NT + 8)
            v_.tensor_copy(dest[:], dest_f[:]).then_inc(payload_ready, 1)
            def elo(u, off):
                dve.wait_ge(ehi_done, u * STEP + (off + 1))
                v_.tensor_tensor(lo[:, half_of(off), :], raw[:, slot_of(off), :], hi[:, half_of(off), :].bitcast(F32),
                                 ALU.subtract).then_inc(elo_done, 1)

            def xe_low(v):
                dve.wait_ge(xe_hi, v + 1)
                v_.tensor_tensor(xel[:].rearrange("p (b c) n -> p b (c n)", b=2), ps[:, 6:8, 0:4 * CAP],
                                 xeh[:].rearrange("p (b c) n -> p b (c n)", b=2).bitcast(F32), ALU.subtract)\
                  .then_inc(xe_lo, 1)

            pairs = ps[0:CAP, 0:4, :].rearrange("p b (n two) -> p (b n) two", two=2)

            def clip_g(v):
                dve.wait_ge(gu_done, v + 1)
                at_least(dve, act_turned, v)
                v_.tensor_scalar(g_lin, pairs[:, :, 0], LIMIT, None, ALU.min).then_inc(g_clip, 1)

            def clip_u(v):
                v_.tensor_scalar(u_lin, pairs[:, :, 1], LIMIT, -LIMIT, ALU.min, ALU.max).then_inc(u_clip, 1)

            def aT_low(v):
                dve.wait_ge(aT_hi, v + 1)
                v_.tensor_tensor(aTl[:].rearrange("p (b c) n -> p b (c n)", b=2), ps[:, 6:8, 0:4 * CAP],
                                 aTh[:].rearrange("p (b c) n -> p b (c n)", b=2).bitcast(F32), ALU.subtract)\
                  .then_inc(aT_lo, 1)

            def bias_low(c0, c1):
                dve.wait_ge(bias_hi, 1)
                v_.tensor_tensor(bias[E:2 * E, c0:c1], bias_raw[E:2 * E, c0:c1], bias[E:2 * E, c0:c1].bitcast(F32),
                                 ALU.subtract).then_inc(bias_lo, 1)

            elo(0, 0)
            v_.tensor_tensor(over[:].rearrange("p (e b) -> p e b", e=E),
                             cnt[:].unsqueeze(2).to_broadcast([P, E, BLOCKS - 1]),
                             limit[:].rearrange("p (e b) -> p e b", e=E), ALU.is_gt).then_inc(extra_step, 1)
            dve.wait_ge(extra_step, 1)
            v_.tensor_tensor_scan(rank[:], picked[:], over[:], 0.0, ALU.mult, ALU.add).then_inc(extra_step, 1)
            dve.wait_ge(extra_step, 2)
            v_.scalar_tensor_tensor(picked[:], rank[:], rank_id[:, 0:1], over[:], ALU.is_equal, ALU.mult)
            v_.tensor_copy(found[:, 2:3], rank[:, CAND - 1:CAND]).then_inc(extra_step, 1)
            dve.wait_ge(extra_step, 3)
            v_.tensor_tensor(pick2[:], picked[:].unsqueeze(1).to_broadcast([P, 2, CAND]), code[:], ALU.mult)\
              .then_inc(extra_step, 1)
            dve.wait_ge(extra_step, 4)
            v_.tensor_reduce(found[:, 0:2], pick2[:], AX_X, ALU.add).then_inc(extra_fill, 1)
            bias_low(0, F2)
            xe_low(0)
            dve.wait_ge(extra_mm, 1)
            v_.tensor_copy(extra_list[:], ps[0:1, 4, 0:3 * P].rearrange("p (a n) -> p a n", a=3)[:, :, 0:32])\
              .then_inc(extra_ready, 1)
            for k in range(1, DOWN):
                elo(0, k)
                if k == 2:
                    bias_low(F2, F2 + D)
            elo(1, -4)
            dve.wait_ge(bias_lo, 2)
            clip_g(0)
            clip_u(0)
            xe_low(1)
            elo(1, -3)

            def step(u, first=False, last=False):
                for k in range(2 if first else 0, 4):
                    elo(u, k - 4)
                aT_low(u - 1)
                for k in range(4, 10):
                    elo(u, k - 4)
                clip_g(u)
                elo(u, 6)
                clip_u(u)
                elo(u, 7)
                if not last:
                    xe_low(u + 1)

            step(1, first=True)
            with dve.Fori(2, E - 1) as u:
                step(u)
            step(E - 1, last=True)
            for k in range(SPLIT):
                elo(E, k - 4)
            aT_low(E - 1)

            def combine(t):
                yt = ytile[t]
                dve.wait_ge(yt_in[t], 16)
                v_.tensor_tensor(yt[:, 0:D], yt[:, 0:D], yt[:, D:2 * D], ALU.add).then_inc(comb, 1)
                dve.wait_ge(comb, 3 * t + 1)
                v_.tensor_tensor(X[:, t, :], X[:, t, :], yt[:, 0:D], ALU.add).then_inc(comb, 1)
                dve.wait_ge(comb, 3 * t + 2)
                dve.wait_ge(pair_sum, t + 1)
                v_.tensor_tensor(X[:, t, :], X[:, t, :], yt[:, 3 * D:], ALU.add).then_inc(comb, 1)

            combine(0)
            combine(1)
            elo(E, SPLIT - 4)
            combine(2)
            combine(3)
            dve.wait_ge(comb, 3 * NT)
            n_extra = dve.value_load(extra_list[0:1, 2, 0:1], min_val=0, max_val=EXTRA)
            with dve.If(0 < n_extra):
                with dve.Fori(0, EXTRA) as i:
                    with dve.If(i < n_extra):
                        v = i + E
                        xe_low(v)
                        for k in range(DOWN):
                            elo(v, k)
                        clip_g(v)
                        clip_u(v)
                        for k in range(DOWN, STEP - 1):
                            elo(v, k)
                        aT_low(v)
                        elo(v, STEP - 1)
                for t in range(NT):
                    dve.wait_ge(extra_in, 16 * NT)
                    for k in range(TOPE):
                        if t or k:
                            dve.wait_ge(extra_added, TOPE * t + k)
                        v_.tensor_tensor(X[:, t, :], X[:, t, :], ytile[t][:, k * D:(k + 1) * D], ALU.add)\
                          .then_inc(extra_added, 1)
                dve.wait_ge(extra_added, TOPE * NT)

            def finish(t):
                dve.wait_ge(rstd_ready, 2 * NT + t + 1)
                dve.wait_ge(gfin_in, 16)
                v_.scalar_tensor_tensor(o_rows[:, t, :], X[:, t, :], rstd[:, 2, t:t + 1], g_fin,
                                        ALU.mult, ALU.mult).then_inc(o_ready, 1)

            dve.wait_ge(late0_in, 16)
            v_.tensor_tensor(X[:], X[:], late_rows[0], ALU.add).then_inc(late_sum, 1)
            dve.wait_ge(late_sum, 1)
            for t in range(NT):
                dve.wait_ge(late1_in[t], 16)
                v_.tensor_tensor(X[:, t, :], X[:, t, :], late_rows[1][:, t, :], ALU.add).then_inc(late_sum, 1)
                if t >= 1:
                    finish(t - 1)
            dve.wait_ge(late_sum, NT + 1)
            finish(NT - 1)

        @block.tensor
        def _(pe):
            m_ = nc.tensor.matmul

            def three(o, ah, al, bh, bl, start, stop):
                m_(o, ah, bh, start=start, stop=False)
                m_(o, ah, bl, start=False, stop=False)
                return m_(o, al, bh, start=False, stop=stop)

            pe.wait_ge(id_step, 2)
            def turn_h(c):
                if c >= 4:
                    pe.wait_ge(xT_lo, c - 3)
                for t in range(NT):
                    if c == 0:
                        pe.wait_ge(h_ready, t + 1)
                    last = nc.tensor.transpose(ps[:, 4 + c % 4, t * P:(t + 1) * P], hN[:, t, c * P:(c + 1) * P], ident[:])
                last.then_inc(h_turned, 1)

            for c in range(4):
                turn_h(c)

            def turn_values():
                pe.wait_ge(evac_dve, 8)
                for t in range(NT):
                    nc.tensor.transpose(ps[:, 6, t * DH:(t + 1) * DH], vT[DH:2 * DH, t * P:(t + 1) * P],
                                        ident[DH:2 * DH, DH:2 * DH])
                for t in range(NT):
                    last = nc.tensor.transpose(ps[:, 6, 256 + t * NI:256 + (t + 1) * NI],
                                               vT[DI:DI + NI, t * P:(t + 1) * P], ident[DI:DI + NI, DI:DI + NI])
                last.then_inc(v_turned, 1)

            def index_products(t, h):
                n = 2 * (t - 1) + h
                if n:
                    pe.wait_ge(relu_done, n)
                nk = P * (t + 1)
                for j in range(4):
                    r = slice(j * DI, (j + 1) * DI)
                    last = m_(ps[:, 2 + j, 0:nk], iqT[r, h, t * P:(t + 1) * P], ikT[r, 0:nk], start=True, stop=True)
                last.then_inc(idx_done, 1)

            def logits(a):
                t, g = attn[a]
                nk = P * (t + 1)
                if a:
                    pe.wait_ge(masked, a)
                else:
                    pe.wait_ge(relu_done, 2 * (NT - 1))
                for j in range(4):
                    h = 4 * g + j
                    r = slice(DH * (h % 2), DH * (h % 2) + DH)
                    last = m_(ps[:, 2 + j, 0:nk], qT[r, h // 2, t * P:(t + 1) * P], kT[r, 0:nk], start=True, stop=True)
                last.then_inc(logits_done, 1)

            for i in range(N_AHEAD):
                pe.wait_ge(lo_done, i + 1)
                if 2 <= i < U_PIECE + 2:
                    pe.wait_ge(evac_dve, i - 1)
                if i >= U_PIECE + 2:
                    pe.wait_ge(evac_act, i - U_PIECE - 1)
                wh, wl = split_piece(whi, i), split_piece(wlo, i)
                for c in range(KC):
                    if i == 0:
                        pe.wait_ge(xT_lo, c + 1)
                        if c + 4 < KC:
                            turn_h(c + 4)
                    last = three(ps[:, i % 2, :], wh[:, c, :], wl[:, c, :], xTh[:, c, :], xTl[:, c, :],
                                 c == 0, c == KC - 1)
                last.then_inc(piece_done, 1)
                if i == U_PIECE:
                    turn_values()
                if 9 <= i < 9 + 2 * (NT - 1):
                    index_products(1 + (i - 9) // 2, (i - 9) % 2)
                if i == FIRST_LOGITS:
                    logits(0)
            pe.wait_ge(evac_act, N_AHEAD - U_PIECE)
            def weigh(a, n):
                t, g = attn[a]
                kb = n - blocks_to[a]
                pe.wait_ge(pT_out, n + 1)
                if g == 0 and t >= 1 and kb == 0:
                    pe.wait_ge(y_norm, t)
                for j in range(4):
                    h = 4 * g + j
                    last = m_(ps[:, 1, h * DH:(h + 1) * DH], pT[:, n % 2, j * P:(j + 1) * P], v_sb[:, kb, :],
                              start=(g == 0 and kb == 0 and j == 0), stop=(kb == t), skip_group_check=True)
                last.then_inc(pv_done, 1)

            def turn_y(t):
                pe.wait_ge(y_norm, t + 1)
                pe.wait_ge(evac_act, N_AHEAD - U_PIECE + 2 * t + 2)
                for c in range(4):
                    last = nc.tensor.transpose(ps[:, 0, c * P:(c + 1) * P], yN[:, c * P:(c + 1) * P], ident[:])
                last.then_inc(y_turned, 1)

            def piece_part(a, c0, c1):
                t, g = attn[a]
                i = N_AHEAD + a
                if c0 == 0:
                    pe.wait_ge(lo_done, i + 1)
                    pe.wait_ge(evac_act, i - U_PIECE)
                    if g == 0 and t >= 1:
                        pe.wait_ge(y_kept, t)
                wh, wl = split_piece(whi, i), split_piece(wlo, i)
                for c in range(c0, c1):
                    last = three(ps[:, 0, :], wh[:, c, :], wl[:, c, :], xTh[:, c, :], xTl[:, c, :],
                                 c == 0, c == KC - 1)
                if c1 == KC:
                    last.then_inc(piece_done, 1)

            for a, (t, g) in enumerate(attn):
                if a + 1 < len(attn):
                    logits(a + 1)
                with_y = g == 0 and t >= 1
                if with_y:
                    turn_y(t - 1)
                else:
                    piece_part(a, 0, KC // 2)
                pe.wait_ge(exp_done, a + 1)
                for n in range(blocks_to[a], blocks_to[a + 1]):
                    if n >= 2:
                        pe.wait_ge(pT_out, n - 1)
                    kb = n - blocks_to[a]
                    for j in range(4):
                        last = nc.tensor.transpose(ps[:, 6 + n % 2, j * P:(j + 1) * P],
                                                   prob[:, a % 2, j, kb * P:(kb + 1) * P], ident[:])
                    last.then_inc(p_turned, 1)
                    if n > blocks_to[a]:
                        weigh(a, n - 1)
                piece_part(a, 0 if with_y else KC // 2, KC)
                weigh(a, blocks_to[a + 1] - 1)
            pe.wait_ge(masked, len(attn))
            for j in range(NG):
                pe.wait_ge(pooled, j + 1)
                m_(ps[:, 2 + j, :], wp[:, j, :], uT[:, j, PAD:], start=True, stop=True).then_inc(pool_mixed, 1)
            turn_y(NT - 1)
            pe.wait_ge(pool_lo, NG)
            pe.wait_ge(y_lo, 2)
            for m in range(N_UP):
                i = N_PROJ + m
                pe.wait_ge(lo_done, i + 1)
                if m >= 2:
                    pe.wait_ge(gated_p, m - 1)
                wh, wl = split_piece(whi, i), split_piece(wlo, i)
                for c in range(KC):
                    last = three(ps[:, 2 * (m % 2) + c // 4, :], wh[:, c, :], wl[:, c, :], xTh[:, c, :], xTl[:, c, :],
                                 c % 4 == 0, c % 4 == 3)
                last.then_inc(piece_done, 1)

            def turn_x2(c, t):
                return nc.tensor.transpose(ps[:, turn_bank(c), t * P:(t + 1) * P], X[:, t, c * P:(c + 1) * P], ident[:])

            def route_chunk(c):
                pe.wait_ge(h2T_dve if c % 2 else h2T_act, c // 2 + 1)
                return m_(ps[0:E, 4, :], wr[:, c, :], h2T(c), start=(c == 0), stop=(c == KC - 1))

            for n in range(2):
                for j in range(4):
                    i = N_PROJ + N_UP + 4 * n + j
                    pe.wait_ge(lo_done, i + 1)
                    pe.wait_ge(mT_lo, 2 * j + 2)
                    wh, wl = split_piece(whi, i), split_piece(wlo, i)
                    for cc in range(2):
                        c = 2 * j + cc
                        for t in range(NT):
                            r = slice(t * P, (t + 1) * P)
                            last = three(ps[:, 4 - 4 * n + t, :], mTh[:, c, r], mTl[:, c, r], wh[:, cc, :], wl[:, cc, :],
                                         c == 0, c == KC - 1)
                    last.then_inc(piece_done, 1)
                    if n == 1 and j == 1:
                        pe.wait_ge(x2_left, 1)
                        for c in range(KC // 2):
                            for t in range(NT):
                                last = turn_x2(c, t)
                            last.then_inc(h2_turned, 1)
                    if n == 1 and j == 2:
                        pe.wait_ge(wr_scaled, 1)
                        for c in range(KC // 2):
                            route_chunk(c)
                pe.wait_ge(piece_done, N_PROJ + N_UP + 4 * n + 4)
                pe.sem_inc(out_mm, 1)
            for t in range(NT):
                pe.wait_ge(x2_right, t + 1)
                for c in range(KC // 2, KC):
                    last = turn_x2(c, t)
                    if t == NT - 1:
                        last.then_inc(h2_turned, 1)
            for c in range(KC // 2, KC):
                last = route_chunk(c)
            last.then_inc(router_mm, 1)
            pe.wait_ge(logits_out, 1)
            for t in range(NT):
                last = nc.tensor.transpose(ps[:, 1, t * E:(t + 1) * E], t_po[0:E, t * P:(t + 1) * P], ident[0:E, 0:E])
            last.then_inc(logits_turned, 1)
            pe.wait_ge(mask_ready, 1)
            for t in range(NT + 1):
                o = ps[:, 7, t * E:(t + 1) * E]
                before = min(t, NT)
                for j in range(before):
                    last = m_(o, ones[:], mask[:, j, :], start=(j == 0), stop=(t == NT and j == NT - 1))
                if t < NT:
                    last = m_(o, tri[:], mask[:, t, :], start=(t == 0), stop=True)
            last.then_inc(pos_mm, 1)
            for e in range(2):
                pe.wait_ge(start_step, e + 2)
                for t in range(NT):
                    last = m_(ps[0:CAP, 5, e:e + 1], start_sel[:, e, t, :], start_tok[:, e, t:t + 1],
                              start=(t == 0), stop=(t == NT - 1))
            last.then_inc(start_mm, 1)
            def turn_rows(v):
                pe.wait_ge(rows_in, v * 16 + 16)
                at_least(pe, aT_lo, v - 1) if isinstance(v, int) else None
                for c in range(KC):
                    last = nc.tensor.transpose(ps[:, 6 + c // 4, (c % 4) * CAP:(c % 4 + 1) * CAP],
                                               xy[:, c * P:(c + 1) * P], ident[0:CAP, 0:CAP])
                last.then_inc(rows_turned, 1)

            def turn_act(v):
                pe.wait_ge(act_ready, v + 1)
                for c in range(KC):
                    last = nc.tensor.transpose(ps[:, 6 + c // 4, (c % 4) * CAP:(c % 4 + 1) * CAP],
                                               g_act[:, c * P:(c + 1) * P], ident[0:CAP, 0:CAP])
                last.then_inc(act_turned, 1)

            def up_bias(v):
                pe.wait_ge(sel_up_ready, v + 1)
                for n in range(4):
                    last = m_(ps[0:CAP, n, :], sel_up[:], bias[:, n * 512:(n + 1) * 512], start=True, stop=False)
                last.then_inc(up_bias_used, 1)

            def up_chunk(u, off, k):
                pe.wait_ge(elo_done, u * STEP + (off + 1))
                h = half_of(off)
                for n in range(4):
                    c = slice(n * 512, (n + 1) * 512)
                    last = three(ps[0:CAP, n, :], xeh[:, k, :], xel[:, k, :], hi[:, h, c], lo[:, h, c],
                                 False, k == DOWN - 1)
                last.then_inc(chunk_used, 1)

            def down_bias(v):
                pe.wait_ge(sel_down_ready, v + 1)
                at_least(pe, y_scaled, v)
                for n in range(2):
                    last = m_(ps[0:CAP, 4 + n, :], sel_down[:], bias[:, F2 + n * 512:F2 + (n + 1) * 512],
                              start=True, stop=False)
                last.then_inc(down_bias_used, 1)

            def down_chunk(u, off, k):
                pe.wait_ge(elo_done, u * STEP + (off + 1))
                h = half_of(off)
                for cc in range(2):
                    for n in range(2):
                        c = slice(cc * D + n * 512, cc * D + (n + 1) * 512)
                        last = three(ps[0:CAP, 4 + n, :], aTh[:, 2 * k + cc, :], aTl[:, 2 * k + cc, :],
                                     hi[:, h, c], lo[:, h, c], False, k == 3 and cc == 1)
                last.then_inc(chunk_used, 1)

            def product_done(which, u, off):
                pe.wait_ge(chunk_used, u * STEP + (off + 1))
                pe.sem_inc(which, 1)

            pe.wait_ge(extra_fill, 1)
            for j in range(3):
                last = m_(ps[0:1, 4, j * P:(j + 1) * P], found[:, j:j + 1], ident[:], start=True, stop=True)
            last.then_inc(extra_mm, 1)
            turn_rows(0)
            pe.wait_ge(bias_lo, 1)
            pe.wait_ge(xe_lo, 1)
            up_bias(0)
            for k in range(DOWN):
                if k == 5:
                    turn_rows(1)
                up_chunk(0, k, k)
            product_done(gu_done, 0, DOWN - 1)

            def step(u, last=False):
                pe.wait_ge(xe_lo, u + 1)
                pe.wait_ge(u_clip, u)
                up_bias(u)
                for k in range(DOWN):
                    if k == 2:
                        turn_act(u - 1)
                    up_chunk(u, k - 4, k)
                product_done(gu_done, u, DOWN - 1 - 4)
                pe.wait_ge(aT_lo, u)
                down_bias(u - 1)
                for k in range(4):
                    if k == 1 and not last:
                        turn_rows(u + 1)
                    down_chunk(u, k + 4, k)
                product_done(down_done, u, DOWN - 1)

            pe.wait_ge(extra_ready, 1)
            pe.wait_ge(bias_lo, 2)
            step(1)
            with pe.Fori(2, E - 1) as u:
                step(u)
            step(E - 1, last=True)
            turn_act(E - 1)
            pe.wait_ge(aT_lo, E)
            down_bias(E - 1)
            for k in range(4):
                down_chunk(E, k - 4, k)
            product_done(down_done, E, -1)
            n_extra = pe.value_load(extra_list[0:1, 2, 0:1], min_val=0, max_val=EXTRA)
            with pe.If(0 < n_extra):
                with pe.Fori(0, EXTRA) as i:
                    with pe.If(i < n_extra):
                        v = i + E
                        turn_rows(v)
                        pe.wait_ge(xe_lo, v + 1)
                        pe.wait_ge(u_clip, v)
                        up_bias(v)
                        for k in range(DOWN):
                            up_chunk(v, k, k)
                        product_done(gu_done, v, DOWN - 1)
                        turn_act(v)
                        pe.wait_ge(aT_lo, v + 1)
                        down_bias(v)
                        for k in range(4):
                            down_chunk(v, k + DOWN, k)
                        product_done(down_done, v, STEP - 1)


_INS = ["x", "norm_mix", "w_in", "w_pool", "pool_scale", "w_attn_up", "w_pool_up", "w_out", "norm_ffn",
        "w_router", "b_router", "w_gate_up", "b_gate_up", "w_down", "b_down", "norm_final"]


def kernel(**inputs):
    import numpy as _np
    import concourse.bacc as _bacc
    from concourse.bass_utils import run_bass_kernel_spmd as _run

    nc = _bacc.Bacc("TRN2", target_bir_lowering=False, num_devices=1)
    arrays, args = {}, []
    for name in _INS:
        a = _np.ascontiguousarray(inputs[name])
        arrays[f"in_{name}_dram"] = a
        args.append(nc.dram_tensor(f"in_{name}_dram", a.shape, mybir.dt.from_np(a.dtype), kind="ExternalInput").ap())
    _, t, d = inputs["x"].shape
    e = inputs["w_router"].shape[2]
    blocks = -(-t // CAP)
    args.append(nc.dram_tensor("h2_dram", (t, d), F32, kind="Internal").ap())
    args.append(nc.dram_tensor("table_dram", (blocks * CAP * e, 4), U32, kind="Internal").ap())
    args.append(nc.dram_tensor("y_dram", (t * TOPE + CAP, d), F32, kind="Internal").ap())
    for name in ("late0_dram", "late1_dram"):
        args.append(nc.dram_tensor(name, (t + CAP, d), F32, kind="Internal").ap())
    args.append(nc.dram_tensor("extra_dram", (t * TOPE + CAP, d), F32, kind="Internal").ap())
    args.append(nc.dram_tensor("out_dram", inputs["x"].shape, F32, kind="ExternalOutput").ap())
    hybrid_block(nc, *args)
    r = _run(nc, [arrays], core_ids=[0])
    return r.results[0]["out_dram"]
```
